# Optimizing a Trainium2 kernel written in Bass

```python
import math
import jax
import jax.numpy as jnp
from jax import lax
import numpy as np
import jax, jax.numpy as jnp

D_MODEL = 1024
BATCH = 1
SEQ = 256
DEPTH = 1

D_PLE = 256
RWKV_WIDTH = D_MODEL // 2
RWKV_HEAD = 64
RWKV_HEADS = RWKV_WIDTH // RWKV_HEAD
DECAY_LORA = 64
AAA_LORA = 64
GATE_LORA = 128
GN_EPS = RWKV_HEAD * 1e-5
DIFF_WIDTH = D_MODEL // 2
DIFF_HEADS = 4
DIFF_HEAD_DIM = DIFF_WIDTH // DIFF_HEADS // 2
SUBLN_EPS = 1e-5
Q_BLOCK = 128
D_FF = 4 * D_MODEL
NORM_EPS = 1e-6
RWKV_COLS = 3 * RWKV_WIDTH + DECAY_LORA + AAA_LORA + GATE_LORA
ATTN_COLS = 3 * DIFF_WIDTH
GATE_COLS = 2 * D_MODEL
IN_COLS = RWKV_COLS + ATTN_COLS + GATE_COLS


def rmsnorm(x, g, eps=NORM_EPS):
    xf = x.astype(jnp.float32)
    y = xf * lax.rsqrt(jnp.mean(xf * xf, axis=-1, keepdims=True) + eps)
    return (y * g.astype(jnp.float32)).astype(x.dtype)

def wkv7_scan(r, w, k, v, a, b):
    bsz, _, nh, n = r.shape

    def step(state, inp):
        r_t, w_t, k_t, v_t, a_t, b_t = inp
        sa = jnp.einsum('bhvk,bhk->bhv', state, a_t)
        state = (state * w_t[:, :, None, :]
                 + sa[..., None] * b_t[:, :, None, :]
                 + v_t[..., None] * k_t[:, :, None, :])
        y_t = jnp.einsum('bhvk,bhk->bhv', state, r_t)
        return state, y_t

    xs = tuple(jnp.moveaxis(t, 1, 0) for t in (r, w, k, v, a, b))
    state0 = jnp.zeros((bsz, nh, n, n), jnp.float32)
    _, ys = lax.scan(step, state0, xs)
    return jnp.moveaxis(ys, 0, 1)

def rwkv7_time_mix(cols, mu, w0, w2, a0, a2, g2, k_k, k_a, r_k, lnx_w, lnx_b):
    out_dtype = cols.dtype
    c = cols.astype(jnp.float32)
    bsz, seq, _ = c.shape
    prev = jnp.pad(c[:, :-1], ((0, 0), (1, 0), (0, 0)))
    c = c + (prev - c) * mu.astype(jnp.float32)
    o1 = RWKV_WIDTH
    o2 = 2 * RWKV_WIDTH
    o3 = 3 * RWKV_WIDTH
    o4 = o3 + DECAY_LORA
    o5 = o4 + AAA_LORA
    r, k, v, wd, ad, gd = jnp.split(c, [o1, o2, o3, o4, o5], axis=-1)
    f32 = lambda t: t.astype(jnp.float32)
    w = -jax.nn.softplus(-(f32(w0) + jnp.tanh(wd) @ f32(w2))) - 0.5
    decay = jnp.exp(-jnp.exp(w))
    a = jax.nn.sigmoid(f32(a0) + ad @ f32(a2))
    g = jax.nn.sigmoid(gd) @ f32(g2)
    heads = lambda t: t.reshape(bsz, seq, RWKV_HEADS, RWKV_HEAD)
    kk = heads(k * f32(k_k))
    kk = kk / jnp.maximum(jnp.sqrt(jnp.sum(kk * kk, axis=-1, keepdims=True)), 1e-12)
    k = k * (1.0 + (a - 1.0) * f32(k_a))
    r_h, k_h, v_h, a_h, w_h = heads(r), heads(k), heads(v), heads(a), heads(decay)
    y = wkv7_scan(r_h, w_h, k_h, v_h, -kk, kk * a_h)
    mean = jnp.mean(y, axis=-1, keepdims=True)
    var = jnp.mean(jnp.square(y - mean), axis=-1, keepdims=True)
    y = (y - mean) * lax.rsqrt(var + GN_EPS)
    y = y.reshape(bsz, seq, RWKV_WIDTH) * f32(lnx_w) + f32(lnx_b)
    bonus = jnp.sum(r_h * k_h * f32(r_k), axis=-1, keepdims=True) * v_h
    y = (y + bonus.reshape(bsz, seq, RWKV_WIDTH)) * g
    return y.astype(out_dtype)

def diff_attention(cols, lam_q1, lam_k1, lam_q2, lam_k2, subln_g, lambda_init):
    out_dtype = cols.dtype
    bsz, seq, _ = cols.shape
    q, k, v = jnp.split(cols.astype(jnp.float32), 3, axis=-1)
    q = q.reshape(bsz, seq, DIFF_HEADS, 2, DIFF_HEAD_DIM) * (DIFF_HEAD_DIM ** -0.5)
    k = k.reshape(bsz, seq, DIFF_HEADS, 2, DIFF_HEAD_DIM)
    v = v.reshape(bsz, seq, DIFF_HEADS, 2 * DIFF_HEAD_DIM)
    f32 = lambda t: t.astype(jnp.float32)
    lam = (jnp.exp(jnp.sum(f32(lam_q1) * f32(lam_k1)))
           - jnp.exp(jnp.sum(f32(lam_q2) * f32(lam_k2))) + lambda_init)
    slopes = 2.0 ** (-8.0 * jnp.arange(1, DIFF_HEADS + 1, dtype=jnp.float32) / DIFF_HEADS)
    outs = []
    for blk in range(seq // Q_BLOCK):
        q0 = blk * Q_BLOCK
        kend = q0 + Q_BLOCK
        qb = q[:, q0:kend]
        kb = k[:, :kend]
        vb = v[:, :kend]
        s = jnp.einsum('bqhcd,bkhcd->bhcqk', qb, kb)
        dist = (q0 + jnp.arange(Q_BLOCK))[:, None] - jnp.arange(kend)[None, :]
        s = s - slopes[None, :, None, None, None] * dist.astype(jnp.float32)
        s = jnp.where(dist >= 0, s, -jnp.inf)
        pr = jax.nn.softmax(s, axis=-1)
        attn = pr[:, :, 0] - lam * pr[:, :, 1]
        outs.append(jnp.einsum('bhqk,bkhe->bqhe', attn, vb))
    o = jnp.concatenate(outs, axis=1)
    o = rmsnorm(o, subln_g, SUBLN_EPS) * (1.0 - lambda_init)
    return o.reshape(bsz, seq, DIFF_WIDTH).astype(out_dtype)

def first_inputs(seed: int = 0) -> dict:
    key = jax.random.key(seed)
    ks = jax.random.split(key, 32)
    L = DEPTH
    nrm = lambda k, shape, scale: jax.random.normal(k, shape, jnp.float32) * scale
    gain = lambda k, shape: 1.0 + 0.05 * jax.random.normal(k, shape, jnp.float32)
    return {
        "x": nrm(ks[0], (BATCH, SEQ, D_MODEL), 1.0),
        "p": nrm(ks[1], (DEPTH, BATCH, SEQ, D_PLE), 1.0),
        "norm_mix_g": gain(ks[2], (L, D_MODEL)),
        "w_in": nrm(ks[3], (L, D_MODEL, IN_COLS), D_MODEL ** -0.5),
        "rwkv_mu": jax.random.uniform(ks[4], (L, RWKV_COLS), jnp.float32),
        "rwkv_w0": jax.random.uniform(ks[5], (L, RWKV_WIDTH), jnp.float32, minval=-4.0, maxval=1.0),
        "rwkv_w2": nrm(ks[6], (L, DECAY_LORA, RWKV_WIDTH), 0.1 * DECAY_LORA ** -0.5),
        "rwkv_a0": nrm(ks[7], (L, RWKV_WIDTH), 0.1),
        "rwkv_a2": nrm(ks[8], (L, AAA_LORA, RWKV_WIDTH), 0.1 * AAA_LORA ** -0.5),
        "rwkv_g2": nrm(ks[9], (L, GATE_LORA, RWKV_WIDTH), GATE_LORA ** -0.5),
        "rwkv_k_k": 0.85 + 0.05 * jax.random.normal(ks[10], (L, RWKV_WIDTH), jnp.float32),
        "rwkv_k_a": gain(ks[11], (L, RWKV_WIDTH)),
        "rwkv_r_k": nrm(ks[12], (L, RWKV_HEADS, RWKV_HEAD), 0.1),
        "rwkv_lnx_w": gain(ks[13], (L, RWKV_WIDTH)),
        "rwkv_lnx_b": nrm(ks[14], (L, RWKV_WIDTH), 0.01),
        "lam_q1": nrm(ks[15], (L, DIFF_HEAD_DIM), 0.1),
        "lam_k1": nrm(ks[16], (L, DIFF_HEAD_DIM), 0.1),
        "lam_q2": nrm(ks[17], (L, DIFF_HEAD_DIM), 0.1),
        "lam_k2": nrm(ks[18], (L, DIFF_HEAD_DIM), 0.1),
        "diff_subln_g": gain(ks[19], (L, 2 * DIFF_HEAD_DIM)),
        "w_proj_a": nrm(ks[20], (L, RWKV_WIDTH, D_MODEL), RWKV_WIDTH ** -0.5),
        "w_proj_b": nrm(ks[21], (L, DIFF_WIDTH, D_MODEL), DIFF_WIDTH ** -0.5),
        "w_out": nrm(ks[22], (L, D_MODEL, D_MODEL), D_MODEL ** -0.5),
        "norm_mlp_g": gain(ks[23], (L, D_MODEL)),
        "w_ff1": nrm(ks[24], (L, D_MODEL, D_FF), D_MODEL ** -0.5),
        "w_ff2": nrm(ks[25], (L, D_FF, D_MODEL), D_FF ** -0.5),
        "norm_ple_g": gain(ks[26], (L, D_MODEL)),
        "w_ple": nrm(ks[27], (L, D_PLE, D_MODEL), D_PLE ** -0.5),
        "w_ple_gate": nrm(ks[28], (L, D_MODEL, D_MODEL), D_MODEL ** -0.5),
        "final_norm_g": gain(ks[29], (D_MODEL,)),
    }

def first_block(x, p, norm_mix_g, w_in, rwkv_mu, rwkv_w0, rwkv_w2, rwkv_a0, rwkv_a2,
              rwkv_g2, rwkv_k_k, rwkv_k_a, rwkv_r_k, rwkv_lnx_w, rwkv_lnx_b,
              lam_q1, lam_k1, lam_q2, lam_k2, diff_subln_g, w_proj_a, w_proj_b,
              w_out, norm_mlp_g, w_ff1, w_ff2, norm_ple_g, w_ple, w_ple_gate,
              final_norm_g):
    for i in range(DEPTH):
        h = rmsnorm(x, norm_mix_g[i])
        u = h @ w_in[i]
        u_rwkv, u_attn, u_gate = jnp.split(u, [RWKV_COLS, RWKV_COLS + ATTN_COLS], axis=-1)
        o_a = rwkv7_time_mix(u_rwkv, rwkv_mu[i], rwkv_w0[i], rwkv_w2[i], rwkv_a0[i],
                             rwkv_a2[i], rwkv_g2[i], rwkv_k_k[i], rwkv_k_a[i],
                             rwkv_r_k[i], rwkv_lnx_w[i], rwkv_lnx_b[i])
        lambda_init = 0.8 - 0.6 * math.exp(-0.3 * i)
        o_b = diff_attention(u_attn, lam_q1[i], lam_k1[i], lam_q2[i], lam_k2[i],
                             diff_subln_g[i], lambda_init)
        g_a, g_b = jnp.split(jax.nn.sigmoid(u_gate), 2, axis=-1)
        merged = g_a * (o_a @ w_proj_a[i]) + g_b * (o_b @ w_proj_b[i])
        x = x + merged @ w_out[i]
        h = rmsnorm(x, norm_mlp_g[i])
        x = x + jnp.square(jax.nn.relu(h @ w_ff1[i])) @ w_ff2[i]
        gate = jax.nn.sigmoid(rmsnorm(x, norm_ple_g[i]) @ w_ple_gate[i])
        x = x + (p[i] @ w_ple[i]) * gate
    return rmsnorm(x, final_norm_g)


DEPTH_2 = 2

HEAD_DIM = 64
N_HEADS = D_MODEL // HEAD_DIM
D_MIX = N_HEADS * HEAD_DIM
H_A = N_HEADS // 2
H_B = N_HEADS - H_A
H_C = N_HEADS // 2
H_D = N_HEADS - H_C
D_FF_2 = 256 * ((8 * D_MODEL + 3 * 256 - 1) // (3 * 256))
FFN_RES_WEIGHT = 0.5
MOBA_BLOCK = 256
MOBA_TOPK = 3
MOBA_Q_BLOCK = 64
DILATED_BRANCHES = ((128, 1), (512, 4), (2048, 16))
ROPE_THETA = 10000.0
RMS_EPS = 1e-6
N_EVEN = (DEPTH_2 + 1) // 2
N_ODD = DEPTH_2 // 2


def rms_norm(x, g):
    xf = x.astype(jnp.float32)
    y = xf * lax.rsqrt(jnp.mean(xf * xf, axis=-1, keepdims=True) + RMS_EPS)
    return (y * g.astype(jnp.float32)).astype(x.dtype)

def swiglu(x, w_gate, w_up, w_down):
    return (jax.nn.silu(x @ w_gate) * (x @ w_up)) @ w_down

def rope_tables(seq):
    inv = 1.0 / (ROPE_THETA ** (jnp.arange(0, HEAD_DIM, 2, dtype=jnp.float32) / HEAD_DIM))
    ang = jnp.arange(seq, dtype=jnp.float32)[:, None] * inv[None, :]
    return jnp.cos(ang), jnp.sin(ang)

def apply_rope(x, cos, sin):
    x1, x2 = jnp.split(x, 2, axis=-1)
    c = cos.astype(x.dtype)
    s = sin.astype(x.dtype)
    return jnp.concatenate([x1 * c - x2 * s, x2 * c + x1 * s], axis=-1)

def split_heads(t, n_heads):
    b, s, _ = t.shape
    return t.reshape(b, s, n_heads, HEAD_DIM).transpose(0, 2, 1, 3)

def merge_heads(t):
    b, h, s, d = t.shape
    return t.transpose(0, 2, 1, 3).reshape(b, s, h * d)

def to_query_blocks(t, blk):
    b, h, s = t.shape[:3]
    t = t.reshape(b, h, s // blk, blk, *t.shape[3:])
    return jnp.moveaxis(t, 2, 0)

def from_query_blocks(t):
    n, b, h, blk, d = t.shape
    return jnp.moveaxis(t, 0, 2).reshape(b, h, n * blk, d)

def stick_breaking_attention(q, k, v):
    b, h, s, dh = q.shape
    scale = dh ** -0.5
    kpos = jnp.arange(s)

    def one_block(args):
        q_blk, i = args
        qpos = i * Q_BLOCK + jnp.arange(Q_BLOCK)
        strict = kpos[None, :] < qpos[:, None]
        z = jnp.einsum('bhqd,bhkd->bhqk', q_blk, k).astype(jnp.float32) * scale
        log_keep = jnp.where(strict, jax.nn.log_sigmoid(-z), 0.0)
        suffix = lax.cumsum(log_keep, axis=3, reverse=True)
        between = jnp.concatenate([suffix[..., 1:], jnp.zeros_like(suffix[..., :1])], axis=-1)
        weight = jnp.where(strict, jnp.exp(jax.nn.log_sigmoid(z) + between), 0.0)
        return jnp.einsum('bhqk,bhkd->bhqd', weight.astype(v.dtype), v)

    out = lax.map(one_block, (to_query_blocks(q, Q_BLOCK), jnp.arange(s // Q_BLOCK)))
    return from_query_blocks(out)

def moba_attention(q, k, v):
    b, h, s, dh = q.shape
    scale = dh ** -0.5
    n_kb = -(-s // MOBA_BLOCK)
    pad = n_kb * MOBA_BLOCK - s
    k_pad = jnp.pad(k, ((0, 0), (0, 0), (0, pad), (0, 0)))
    v_pad = jnp.pad(v, ((0, 0), (0, 0), (0, pad), (0, 0)))
    k_blocks = k_pad.reshape(b, h, n_kb, MOBA_BLOCK, dh)
    v_blocks = v_pad.reshape(b, h, n_kb, MOBA_BLOCK, dh)
    k_mean = jnp.mean(k_blocks.astype(jnp.float32), axis=3)
    top_k = min(MOBA_TOPK, n_kb)
    bi = jnp.arange(b)[:, None, None, None]
    hi = jnp.arange(h)[None, :, None, None]
    blk_ids = jnp.arange(n_kb)
    local = jnp.arange(MOBA_BLOCK)
    n_sel = top_k * MOBA_BLOCK

    def one_block(args):
        q_blk, i = args
        q0 = i * MOBA_Q_BLOCK
        qpos = q0 + jnp.arange(MOBA_Q_BLOCK)
        own = q0 // MOBA_BLOCK
        gate = jnp.einsum('bhqd,bhnd->bhqn', q_blk.astype(jnp.float32), k_mean)
        gate = jnp.where(blk_ids < own, gate, -jnp.inf)
        _, sel = lax.top_k(gate, top_k)
        sel_ok = jnp.arange(top_k) < own
        k_sel = k_blocks[bi, hi, sel]
        v_sel = v_blocks[bi, hi, sel]
        s_sel = jnp.einsum('bhqd,bhqnkd->bhqnk', q_blk, k_sel).astype(jnp.float32) * scale
        s_sel = jnp.where(sel_ok[:, None], s_sel, -jnp.inf).reshape(b, h, MOBA_Q_BLOCK, n_sel)
        k_own = lax.dynamic_slice_in_dim(k_pad, own * MOBA_BLOCK, MOBA_BLOCK, axis=2)
        v_own = lax.dynamic_slice_in_dim(v_pad, own * MOBA_BLOCK, MOBA_BLOCK, axis=2)
        s_own = jnp.einsum('bhqd,bhkd->bhqk', q_blk, k_own).astype(jnp.float32) * scale
        s_own = jnp.where(own * MOBA_BLOCK + local[None, :] <= qpos[:, None], s_own, -jnp.inf)
        p = jax.nn.softmax(jnp.concatenate([s_sel, s_own], axis=-1), axis=-1).astype(v.dtype)
        p_sel = p[..., :n_sel].reshape(b, h, MOBA_Q_BLOCK, top_k, MOBA_BLOCK)
        p_own = p[..., n_sel:]
        return (jnp.einsum('bhqnk,bhqnkd->bhqd', p_sel, v_sel)
                + jnp.einsum('bhqk,bhkd->bhqd', p_own, v_own))

    out = lax.map(one_block, (to_query_blocks(q, MOBA_Q_BLOCK), jnp.arange(s // MOBA_Q_BLOCK)))
    return from_query_blocks(out)

def forgetting_attention(q, k, v, log_f):
    b, h, s, dh = q.shape
    scale = dh ** -0.5
    c = jnp.cumsum(log_f, axis=-1)
    kpos = jnp.arange(s)

    def one_block(args):
        q_blk, c_blk, i = args
        qpos = i * Q_BLOCK + jnp.arange(Q_BLOCK)
        logits = (jnp.einsum('bhqd,bhkd->bhqk', q_blk, k).astype(jnp.float32) * scale
                  + c_blk[..., :, None] - c[..., None, :])
        logits = jnp.where(kpos[None, :] <= qpos[:, None], logits, -jnp.inf)
        p = jax.nn.softmax(logits, axis=-1).astype(v.dtype)
        return jnp.einsum('bhqk,bhkd->bhqd', p, v)

    out = lax.map(one_block, (to_query_blocks(q, Q_BLOCK), to_query_blocks(c, Q_BLOCK),
                              jnp.arange(s // Q_BLOCK)))
    return from_query_blocks(out)

def dilated_window_attention(q, k, v):
    b, h, s, dh = q.shape
    scale = dh ** -0.5

    def one_block(args):
        q_blk, i = args
        qpos = i * Q_BLOCK + jnp.arange(Q_BLOCK)
        maxes, denoms, outs = [], [], []
        for window, dil in DILATED_BRANCHES:
            steps = jnp.arange(window // dil + 1)
            kpos = qpos[:, None] - dil * steps[None, :]
            idx = jnp.maximum(kpos, 0)
            k_g = jnp.take(k, idx, axis=2)
            v_g = jnp.take(v, idx, axis=2)
            logits = jnp.einsum('bhqd,bhqnd->bhqn', q_blk, k_g).astype(jnp.float32) * scale
            logits = jnp.where(kpos >= 0, logits, -jnp.inf)
            m = jnp.max(logits, axis=-1, keepdims=True)
            e = jnp.exp(logits - m)
            l = jnp.sum(e, axis=-1, keepdims=True)
            outs.append(jnp.einsum('bhqn,bhqnd->bhqd', e, v_g.astype(jnp.float32)) / l)
            maxes.append(m)
            denoms.append(l)
        m_all = jnp.stack(maxes)
        s_all = jnp.stack(denoms) * jnp.exp(m_all - jnp.max(m_all, axis=0, keepdims=True))
        alpha = s_all / jnp.sum(s_all, axis=0, keepdims=True)
        return jnp.sum(alpha * jnp.stack(outs), axis=0).astype(v.dtype)

    out = lax.map(one_block, (to_query_blocks(q, Q_BLOCK), jnp.arange(s // Q_BLOCK)))
    return from_query_blocks(out)

def mix_stick_moba(xn, w_in, g_q_b, g_k_b, cos, sin):
    q, k, v = jnp.split(xn @ w_in, 3, axis=-1)
    q, k, v = split_heads(q, N_HEADS), split_heads(k, N_HEADS), split_heads(v, N_HEADS)
    out_a = stick_breaking_attention(q[:, :H_A], k[:, :H_A], v[:, :H_A])
    q_b = apply_rope(rms_norm(q[:, H_A:], g_q_b), cos, sin)
    k_b = apply_rope(rms_norm(k[:, H_A:], g_k_b), cos, sin)
    out_b = moba_attention(q_b, k_b, v[:, H_A:])
    return merge_heads(jnp.concatenate([out_a.astype(xn.dtype), out_b.astype(xn.dtype)], axis=1))

def mix_forget_dilated(xn, w_in, b_f, g_q_c, g_k_c, g_q_d, g_k_d, cos, sin):
    proj = xn @ w_in
    q, k, v = jnp.split(proj[..., :3 * D_MIX], 3, axis=-1)
    q, k, v = split_heads(q, N_HEADS), split_heads(k, N_HEADS), split_heads(v, N_HEADS)
    log_f = jax.nn.log_sigmoid((proj[..., 3 * D_MIX:] + b_f).astype(jnp.float32)).transpose(0, 2, 1)
    q_c = rms_norm(q[:, :H_C], g_q_c)
    k_c = rms_norm(k[:, :H_C], g_k_c)
    out_c = forgetting_attention(q_c, k_c, v[:, :H_C], log_f)
    q_d = apply_rope(rms_norm(q[:, H_C:], g_q_d), cos, sin)
    k_d = apply_rope(rms_norm(k[:, H_C:], g_k_d), cos, sin)
    out_d = dilated_window_attention(q_d, k_d, v[:, H_C:])
    return merge_heads(jnp.concatenate([out_c.astype(xn.dtype), out_d.astype(xn.dtype)], axis=1))

def second_inputs(seed: int = 0) -> dict:
    key = jax.random.key(seed)
    ks = jax.random.split(key, 20)

    def normal(k, shape, scale):
        return jax.random.normal(k, shape, jnp.float32) * scale

    def gain(k, shape):
        return 1.0 + 0.02 * jax.random.normal(k, shape, jnp.float32)

    return {
        'x': normal(ks[0], (BATCH, SEQ, D_MODEL), 1.0),
        'norm_ffn1': gain(ks[1], (DEPTH_2, D_MODEL)),
        'ffn1_w_gate': normal(ks[2], (DEPTH_2, D_MODEL, D_FF_2), D_MODEL ** -0.5),
        'ffn1_w_up': normal(ks[3], (DEPTH_2, D_MODEL, D_FF_2), D_MODEL ** -0.5),
        'ffn1_w_down': normal(ks[4], (DEPTH_2, D_FF_2, D_MODEL), D_FF_2 ** -0.5),
        'norm_mix': gain(ks[5], (DEPTH_2, D_MODEL)),
        'w_in_ab': normal(ks[6], (N_EVEN, D_MODEL, 3 * D_MIX), D_MODEL ** -0.5),
        'g_q_b': gain(ks[7], (N_EVEN, HEAD_DIM)),
        'g_k_b': gain(ks[8], (N_EVEN, HEAD_DIM)),
        'w_in_cd': normal(ks[9], (N_ODD, D_MODEL, 3 * D_MIX + H_C), D_MODEL ** -0.5),
        'b_f': normal(ks[10], (N_ODD, H_C), 0.1),
        'g_q_c': gain(ks[11], (N_ODD, HEAD_DIM)),
        'g_k_c': gain(ks[12], (N_ODD, HEAD_DIM)),
        'g_q_d': gain(ks[13], (N_ODD, HEAD_DIM)),
        'g_k_d': gain(ks[14], (N_ODD, HEAD_DIM)),
        'w_out': normal(ks[15], (DEPTH_2, D_MIX, D_MODEL), D_MIX ** -0.5),
        'norm_ffn2': gain(ks[16], (DEPTH_2, D_MODEL)),
        'ffn2_w_gate': normal(ks[17], (DEPTH_2, D_MODEL, D_FF_2), D_MODEL ** -0.5),
        'ffn2_w_up': normal(ks[18], (DEPTH_2, D_MODEL, D_FF_2), D_MODEL ** -0.5),
        'ffn2_w_down': normal(ks[19], (DEPTH_2, D_FF_2, D_MODEL), D_FF_2 ** -0.5),
    }

def second_block(x, norm_ffn1, ffn1_w_gate, ffn1_w_up, ffn1_w_down, norm_mix, w_in_ab, g_q_b, g_k_b,
              w_in_cd, b_f, g_q_c, g_k_c, g_q_d, g_k_d, w_out, norm_ffn2, ffn2_w_gate, ffn2_w_up,
              ffn2_w_down):
    cos, sin = rope_tables(x.shape[1])
    for layer in range(DEPTH_2):
        j = layer // 2
        x = x + FFN_RES_WEIGHT * swiglu(rms_norm(x, norm_ffn1[layer]), ffn1_w_gate[layer],
                                        ffn1_w_up[layer], ffn1_w_down[layer])
        xn = rms_norm(x, norm_mix[layer])
        if layer % 2 == 0:
            mixed = mix_stick_moba(xn, w_in_ab[j], g_q_b[j], g_k_b[j], cos, sin)
        else:
            mixed = mix_forget_dilated(xn, w_in_cd[j], b_f[j], g_q_c[j], g_k_c[j],
                                       g_q_d[j], g_k_d[j], cos, sin)
        x = x + mixed @ w_out[layer]
        x = x + FFN_RES_WEIGHT * swiglu(rms_norm(x, norm_ffn2[layer]), ffn2_w_gate[layer],
                                        ffn2_w_up[layer], ffn2_w_down[layer])
    return x


def setup_inputs(seed=0):
    out = dict(first_inputs(seed))
    for name, value in second_inputs(seed + 1).items():
        if name != "x":
            out[name + "_2"] = value
    return out


def reference(
    x, p, norm_mix_g, w_in, rwkv_mu, rwkv_w0, rwkv_w2, rwkv_a0, rwkv_a2, rwkv_g2, rwkv_k_k,
    rwkv_k_a, rwkv_r_k, rwkv_lnx_w, rwkv_lnx_b, lam_q1, lam_k1, lam_q2, lam_k2, diff_subln_g,
    w_proj_a, w_proj_b, w_out, norm_mlp_g, w_ff1, w_ff2, norm_ple_g, w_ple, w_ple_gate,
    final_norm_g, norm_ffn1_2, ffn1_w_gate_2, ffn1_w_up_2, ffn1_w_down_2, norm_mix_2, w_in_ab_2,
    g_q_b_2, g_k_b_2, w_in_cd_2, b_f_2, g_q_c_2, g_k_c_2, g_q_d_2, g_k_d_2, w_out_2,
    norm_ffn2_2, ffn2_w_gate_2, ffn2_w_up_2, ffn2_w_down_2,
):
    x = first_block(
        x, p, norm_mix_g, w_in, rwkv_mu, rwkv_w0, rwkv_w2, rwkv_a0, rwkv_a2, rwkv_g2, rwkv_k_k,
        rwkv_k_a, rwkv_r_k, rwkv_lnx_w, rwkv_lnx_b, lam_q1, lam_k1, lam_q2, lam_k2,
        diff_subln_g, w_proj_a, w_proj_b, w_out, norm_mlp_g, w_ff1, w_ff2, norm_ple_g, w_ple,
        w_ple_gate, final_norm_g,
    )
    return second_block(
        x, norm_ffn1_2, ffn1_w_gate_2, ffn1_w_up_2, ffn1_w_down_2, norm_mix_2, w_in_ab_2,
        g_q_b_2, g_k_b_2, w_in_cd_2, b_f_2, g_q_c_2, g_k_c_2, g_q_d_2, g_k_d_2, w_out_2,
        norm_ffn2_2, ffn2_w_gate_2, ffn2_w_up_2, ffn2_w_down_2,
    )


_drawn_inputs = setup_inputs


def setup_inputs(seed=0):
    import zlib

    import numpy as np

    out = dict(_drawn_inputs(seed))
    spreads = {}
    factors = {'rwkv_w2': 8.0,
     'rwkv_a0': 3.825,
     'rwkv_a2': 4.428,
     'rwkv_k_k': 7.146,
     'rwkv_k_a': 3.362,
     'rwkv_lnx_w': 3.559,
     'rwkv_lnx_b': 8.0,
     'lam_k1': 2.771,
     'lam_k2': 4.343,
     'norm_ple_g': 8.0,
     'norm_ffn1_2': 4.858,
     'norm_mix_2': 3.583,
     'g_q_b_2': 8.0,
     'g_k_b_2': 8.0,
     'b_f_2': 3.969,
     'g_q_c_2': 8.0,
     'g_k_c_2': 22.07,
     'g_q_d_2': 24.315,
     'g_k_d_2': 23.197,
     'norm_ffn2_2': 5.701}
    for name, (base, spread) in spreads.items():
        noise = np.random.default_rng([zlib.crc32(name.encode()), seed]).standard_normal(out[name].shape)
        drawn = base * np.exp(spread * noise) if base else spread * noise
        out[name] = jnp.asarray(drawn.astype(out[name].dtype))
    for name, factor in factors.items():
        out[name] = (out[name] * factor).astype(out[name].dtype)
    return out
```

```python
import math
from contextlib import ExitStack

import numpy as np

import concourse.bass as bass
from concourse import mybir

F = mybir.dt.float32
R = mybir.dt.float32r
ALU = mybir.AluOpType
ACT = mybir.ActivationFunctionType
AX = mybir.AxisListType

S = 256
D = 1024
EPS = 1e-6
BIG = -1.0e30
GAMMA = math.exp(-0.5)
LN_SHIFT = 30.0 * math.log(2.0)

NRAW = 4
NSPL = 3
PIECE = 2048


def stream_plan():
    plan = []

    def cols(name, layer, kt, c0, n, w):
        for c in range(c0, c0 + n, w):
            plan.append((name, layer, 0, kt, c, w))

    def deep(name, layer, kt, c0, w=1024):
        per = PIECE // w
        for k in range(0, kt, per):
            plan.append((name, layer, k, per, c0, w))

    cols("w_in", 0, 8, 0, 1792, 256)
    cols("w_in", 0, 8, 1792, 1024, 256)
    deep("w_in", 0, 8, 2816, 512)
    cols("w_in", 0, 8, 3328, 2048, 256)
    cols("w_proj_a", 0, 4, 0, 1024, 512)
    cols("w_proj_b", 0, 4, 0, 1024, 512)
    deep("w_out", 0, 8, 0)
    cols("w_ff1", 0, 8, 0, 4096, 256)
    deep("w_ff2", 0, 32, 0)
    deep("w_ple_gate", 0, 8, 0)
    deep("w_ple", 0, 2, 0)

    def ffn(n, layer):
        for c in range(0, 2816, 256):
            cols(f"ffn{n}_w_gate_2", layer, 8, c, 256, 256)
            cols(f"ffn{n}_w_up_2", layer, 8, c, 256, 256)
        deep(f"ffn{n}_w_down_2", layer, 22, 0)

    for layer in range(2):
        ffn(1, layer)
        if layer == 0:
            cols("w_in_ab_2", 0, 8, 0, 512, 256)
            cols("w_in_ab_2", 0, 8, 1024, 512, 256)
            deep("w_in_ab_2", 0, 8, 512, 512)
            deep("w_in_ab_2", 0, 8, 1536, 512)
            deep("w_in_ab_2", 0, 8, 2048)
        else:
            deep("w_in_cd_2", 0, 8, 0, 512)
            deep("w_in_cd_2", 0, 8, 512, 512)
            deep("w_in_cd_2", 0, 8, 1024, 512)
            deep("w_in_cd_2", 0, 8, 1536, 512)
            deep("w_in_cd_2", 0, 8, 2048)
        deep("w_out_2", layer, 8, 0)
        ffn(2, layer)
    return plan


COLS = [("norm_mix_g", 8), ("rwkv_mu", 14), ("rwkv_w0", 4), ("rwkv_a0", 4), ("rwkv_k_k", 4), ("rwkv_k_a", 4),
        ("rwkv_r_k", 4), ("rwkv_lnx_w", 4), ("rwkv_lnx_b", 4), ("diff_subln_g", 1), ("norm_mlp_g", 8),
        ("norm_ple_g", 8), ("norm_ffn1_2", 16), ("norm_mix_2", 16), ("norm_ffn2_2", 16)]


def col_at():
    at, n = {}, 0
    for name, w in COLS:
        at[name] = n
        n += w
    return at, n


CONSTS = [("ident", 128), ("strict", 128), ("incl", 128), ("dgt", 128), ("dgn", 128), ("ofn", 128),
          ("bones", 128), ("ones128", 128), ("ntri", 128), ("nones", 128), ("caus", 384), ("dil", 384),
          ("ndist", 384), ("cos", 128), ("sin", 128), ("eps", 8)]


def const_at():
    at, n = {}, 0
    for name, w in CONSTS:
        at[name] = (n, w)
        n += w
    return at, n


def constants():
    at, n = const_at()
    c = np.zeros((128, n), np.float32)

    def put(name, a):
        o, w = at[name]
        c[:a.shape[0], o:o + w] = a.reshape(a.shape[0], w)

    p = np.arange(128)
    put("ident", np.eye(128))
    put("strict", (p[:, None] < p[None, :]).astype(np.float32))
    put("incl", (p[:, None] <= p[None, :]).astype(np.float32))
    same = (p[:, None] // 16) == (p[None, :] // 16)
    put("dgt", ((p[:, None] < p[None, :]) & same).astype(np.float32))
    put("dgn", ((p[:, None] > p[None, :]) & same).astype(np.float32))
    put("ofn", ((p[:, None] > p[None, :]) & ~same).astype(np.float32))
    put("bones", ((p[:, None] // 64) == (p[None, :] // 64)).astype(np.float32))
    put("ones128", np.ones((128, 128)))
    put("ntri", -(p[:, None] >= p[None, :]).astype(np.float32))
    put("nones", -np.ones((128, 128)))
    d0 = p[:, None] - p[None, :]
    d1 = 128 + p[:, None] - np.arange(256)[None, :]
    dist = np.concatenate([d0, d1], 1)
    ok = dist >= 0
    put("caus", np.where(ok, 0.0, BIG))
    cnt = ((dist <= 128).astype(int) + (dist % 4 == 0) + (dist % 16 == 0)) * ok
    put("dil", np.where(cnt > 0, np.log(np.maximum(cnt, 1)), BIG))
    put("ndist", np.where(ok, -dist, 0))
    inv = 1.0 / (10000.0 ** (np.arange(0, 64, 2, dtype=np.float32) / np.float32(64)))
    ang = (np.arange(256, dtype=np.float32)[:, None] * inv.astype(np.float32)[None, :]).astype(np.float64)
    cs, sn = np.cos(ang), np.sin(ang)
    put("cos", np.concatenate([cs, cs], 1).reshape(2, 128, 64).transpose(1, 0, 2))
    put("sin", np.concatenate([-sn, sn], 1).reshape(2, 128, 64).transpose(1, 0, 2))
    put("eps", np.tile(np.array([EPS, 64 * 1e-5, 1e-5, LN_SHIFT / 2, 1.0, 0, 0, 0]), (128, 1)))
    return c


ROWS = [("final_norm_g", 1024)]
SMALL = [("lam", 256), ("gq", 64), ("gqs", 64), ("gk", 64), ("gks", 64),
         ("gqd", 64), ("gqds", 64), ("gkd", 64), ("gkds", 64), ("gqc", 64), ("gkc", 64),
         ("w2a2", 512), ("g2", 512), ("wf", 64), ("bf", 1)]


def small_at():
    at, n = {}, 0
    for name, w in SMALL:
        at[name] = (n, w)
        n += w
    return at, n


class Engine:

    def __init__(self, sem, linked=False):
        self.sem = sem
        self.linked = linked
        self.n = 0
        self.q = []
        self.passed = {}

    def wait(self, *tokens):
        for t in tokens:
            if t is None:
                continue
            if isinstance(t, list):
                self.wait(*t)
                continue
            sem, value = t
            if self.passed.get(id(sem), 0) < value:
                self.passed[id(sem)] = value
                self.q.append((_wait, (sem, value), {}, None))

    def do(self, f, *a, w=(), inc=True, **k):
        self.wait(*w)
        if self.linked and self.n:
            self.wait((self.sem, self.n))
        self.q.append((f, a, k, (self.sem, 1) if inc else None))
        if inc:
            self.n += 1
            return (self.sem, self.n)
        return None

    def dma(self, out, in_, sem, w=()):
        self.wait(*w)
        self.q.append((_dma, (out, in_), {}, (sem, 16)))

    def replay(self, e):
        for f, a, k, inc in self.q:
            ins = f(e, *a, **k)
            if inc:
                ins.then_inc(inc[0], inc[1])


def _wait(e, sem, value):
    e.wait_ge(sem, value)


def _dma(e, out, in_):
    return e.dma_start(out, in_)


def bc(ap, dim, n):
    shape = list(ap.shape)
    shape[dim] = n
    return ap.broadcast_to(shape)


def act(e, out, in_, func, **k):
    return e.activation(out, in_, func, **k)


def mm(e, out, a, b, start, stop):
    return e.matmul(out, a, b, start=start, stop=stop)


def tr(e, out, a, ident):
    return e.transpose(out, a, ident)


def cp(e, out, a):
    return e.tensor_copy(out, a)


def acopy(e, out, a):
    return e.copy(out, a)


def ts(e, out, a, s1, s2, op0, op1=None):
    if op1 is None:
        return e.tensor_scalar(out, a, s1, None, op0)
    return e.tensor_scalar(out, a, s1, s2, op0, op1)


def tt(e, out, a, b, op):
    return e.tensor_tensor(out, a, b, op)


def stt(e, out, a, s, b, op0, op1):
    return e.scalar_tensor_tensor(out=out, in0=a, scalar=s, in1=b, op0=op0, op1=op1)


def ttr(e, out, a, b, op0, op1, init, acc):
    return e.tensor_tensor_reduce(out, a, b, 1.0, init, op0, op1, acc)


def red(e, out, a, op):
    return e.tensor_reduce(out, a, AX.X, op)


def rcp(e, out, a):
    return e.reciprocal(out, a)


def scan(e, out, d0, d1, init, op0, op1):
    return e.tensor_tensor_scan(out, d0, d1, init, op0, op1)


def mset(e, out, v):
    return e.memset(out, v)


def program(nc, ws, xin, pin, colsin, constin, smallin, rowin, out):
    plan = stream_plan()
    CA, NCOL = col_at()
    KA, NK = const_at()
    SA, NS_ = small_at()
    with ExitStack() as ctx:
        def sem(name):
            return ctx.enter_context(nc.semaphore(name))

        P = Engine(sem("s_pe"))
        V = Engine(sem("s_dve"), linked=True)
        A = Engine(sem("s_act"), linked=True)
        G = Engine(sem("s_pool"))
        SP = Engine(sem("s_sp"))
        s_raw = [sem(f"s_raw{i}") for i in range(NRAW)]
        s_const = sem("s_const")
        s_row = sem("s_row")
        s_out = sem("s_out")

        base = (nc.sbuf_base + 63) // 64 * 64
        top = [base]

        def at(name, shape, dt, offset):
            return nc.alloc_sbuf_tensor_at(name, shape, dt, offset=offset)

        def fixed(name, shape, dt=F):
            size = 4 * int(np.prod(shape[1:]))
            t = at(name, shape, dt, top[0])
            top[0] += (size + 31) // 32 * 32
            return t

        raw = [fixed(f"raw{i}", [128, PIECE]) for i in range(NRAW)]
        hi = [fixed(f"hi{i}", [128, PIECE], R) for i in range(NSPL)]
        lo = [fixed(f"lo{i}", [128, PIECE], R) for i in range(NSPL)]
        X = fixed("X", [128, 2, D])
        HH = fixed("HH", [128, 8, S], R)
        HL = fixed("HL", [128, 8, S], R)
        cols = fixed("cols", [128, NCOL])
        const = fixed("const", [128, NK])
        small = fixed("small", [128, NS_])
        st = fixed("st", [128, 128])
        arena0 = top[0]
        arena_end = nc.sbuf_usable_end
        names = [0]

        class Arena:
            def __init__(self, start=0):
                self.p = arena0 + start

            def __call__(self, shape, dt=F):
                size = 4 * int(np.prod(shape[1:]))
                names[0] += 1
                t = at(f"a{names[0]}", shape, dt, self.p)
                self.p += (size + 31) // 32 * 32
                assert self.p <= arena_end, (self.p - arena0, arena_end - arena0)
                return t

            def here(self):
                return self.p - arena0

        banks = [ctx.enter_context(nc.psum_tensor(f"ps{i}", [128, 512], F)) for i in range(8)]
        free = [(i, []) for i in range(8)]

        def take():
            return free.pop(0)

        def give(i, tokens):
            free.append((i, list(tokens)))

        def K(name, rows=128):
            o, w = KA[name]
            return const[0:rows, o:o + w]

        def SM(name, r0=0, r1=128):
            o, w = SA[name]
            return small[r0:r1, o:o + w]

        def col(name, i=0):
            o = CA[name] + i
            return cols[:, o:o + 1]

        ident = K("ident")

        def cK(name, i):
            o, _ = KA[name]
            return const[:, o + i:o + i + 1]

        eps6, epsgn, epssub, lnsh, one1 = [cK("eps", i) for i in range(5)]

        SP.dma(X[:, :, :], xin, s_const)
        SP.dma(cols[:, :], colsin, s_const)
        SP.dma(const[:, :], constin, s_const)
        SP.dma(small[:, :], smallin, s_const)
        t_const = (s_const, 64)

        raw_tok = {}
        spl_tok = {}
        raw_free = [[] for _ in range(NRAW)]
        issued = [0]
        cursor = [0]
        splits = [0]

        def issue():
            i = issued[0]
            if i >= len(plan):
                return
            s = i % NRAW
            SP.dma(raw[s][:, :], ws[i], s_raw[s], w=raw_free[s])
            raw_tok[i] = (s_raw[s], 16 * (i // NRAW + 1))
            issued[0] += 1

        def split(after):
            i = splits[0]
            if i >= len(plan):
                return
            s = i % NSPL
            r = raw[i % NRAW]
            ta = A.do(acopy, hi[s][:, :], r[:, :], w=[raw_tok[i], after])
            tv = V.do(tt, lo[s][:, :], r[:, :], hi[s][:, :].bitcast(F), ALU.subtract, w=[raw_tok[i], after, ta])
            spl_tok[i] = [ta, tv]
            raw_free[i % NRAW] = [ta, tv]
            splits[0] += 1
            issue()

        for _ in range(NRAW):
            issue()
        for _ in range(NSPL):
            split(None)

        def piece(name, layer, kt, c):
            i = cursor[0]
            n, ly, k0, nk, c0, w = plan[i]
            assert (n, ly, k0, c0) == (name, layer, kt, c), (plan[i], name, layer, kt, c)
            P.wait(spl_tok[i])
            s = i % NSPL
            return (hi[s][:, :].rearrange("p (k n) -> p k n", k=nk),
                    lo[s][:, :].rearrange("p (k n) -> p k n", k=nk))

        def done(tok):
            cursor[0] += 1
            split(tok)

        def mm3(o, ah, al, bh, bl, start, stop):
            P.do(mm, o, ah, bh, start, False, inc=False)
            P.do(mm, o, ah, bl, False, False, inc=False)
            return P.do(mm, o, al, bh, False, stop, inc=stop)

        def proj_t(name, layer, c, sh, sl, w, nk, deps, evac):
            wh, wl = piece(name, layer, 0, c)
            P.wait(*deps)
            got = []
            for j in range(0, w, 256):
                b, fr = take()
                P.wait(fr)
                o = banks[b][:, :].rearrange("p (a n) -> p a n", a=2)
                for u in range(2):
                    for k in range(nk):
                        a, z = j + 128 * u, j + 128 * u + 128
                        t = mm3(o[:, u, :], wh[:, k, a:z], wl[:, k, a:z], sh[:, k, :], sl[:, k, :],
                                k == 0, k == nk - 1)
                got.append((b, o, c + j, t))
            done(got[-1][3])
            for b, o, cc, t in got:
                give(b, evac(o, cc, t))

        def proj_n(name, layer, kts, c, width, sh, sl, deps, evac):
            per = PIECE // width
            nh = width // 512
            bk = [take() for _ in range(2 * nh)]
            for n, k0 in enumerate(range(0, kts, per)):
                wh, wl = piece(name, layer, k0, c)
                P.wait(*deps)
                if n == 0:
                    for _, fr in bk:
                        P.wait(fr)
                for k in range(per):
                    for b in range(2):
                        last = k0 + k == kts - 1
                        for h in range(nh):
                            o = banks[bk[nh * b + h][0]][:, :]
                            ah = sh[:, k0 + k, 128 * b:128 * b + 128]
                            al = sl[:, k0 + k, 128 * b:128 * b + 128]
                            P.do(mm, o, ah, wh[:, k, 512 * h:512 * h + 512], k0 + k == 0, False, inc=False)
                            P.do(mm, o, ah, wl[:, k, 512 * h:512 * h + 512], False, False, inc=False)
                            t = P.do(mm, o, al, wh[:, k, 512 * h:512 * h + 512], False, last)
                done(t)
            for b in range(2):
                for h in range(nh):
                    i = bk[nh * b + h][0]
                    give(i, evac(banks[i][:, :], b, h, t))

        xt = [[t_const], [t_const]]
        h_free = [None]

        def rms_stat(src_tok, scratch):
            ta = A.do(act, scratch[:, 0, :], X[:, 0, :], ACT.Square, accum_out=st[:, 0:1],
                      w=[src_tok[0], t_const])
            tv = V.do(ttr, scratch[:, 1, :], X[:, 1, :], X[:, 1, :], ALU.mult, ALU.add, 0.0, st[:, 1:2],
                      w=[src_tok[1], t_const])
            t1 = A.do(act, st[:, 2:4], st[:, 0:2], ACT.Ln, scale=1.0 / D, bias=eps6, w=[ta, tv])
            return A.do(act, st[:, 4:6], st[:, 2:4], ACT.Exp, scale=-0.5, w=[t1])

        def norm_t(gname, gi, ar):
            xs = ar([128, 2, D])
            tr_ = rms_stat(xt, xs)
            sc = []
            sc.append(V.do(ts, xs[:, 0, :], X[:, 0, :], st[:, 4:5], None, ALU.mult, w=[tr_]))
            sc.append(A.do(act, xs[:, 1, :], X[:, 1, :], ACT.Copy, scale=st[:, 5:6], w=[tr_]))
            toks = []
            for m in range(4):
                b, fr = take()
                P.wait(fr, *sc)
                o = banks[b][:, :].rearrange("p (a n) -> p a n", a=2)
                for u in range(2):
                    for q in range(2):
                        c = 2 * m + u
                        t = P.do(tr, o[:, u, 128 * q:128 * q + 128], xs[:, q, 128 * c:128 * c + 128], ident,
                                 inc=(u == 1 and q == 1))
                rd = []
                for u in range(2):
                    c = 2 * m + u
                    ta = A.do(act, HH[:, c, :], o[:, u, :], ACT.Copy, scale=col(gname, gi + c),
                              w=[t, h_free[0]])
                    rd.append(ta)
                for u in range(2):
                    c = 2 * m + u
                    g = col(gname, gi + c)
                    tv = V.do(stt, HL[:, c, :], o[:, u, :], g, HH[:, c, :].bitcast(F), ALU.mult, ALU.subtract,
                              w=[ta, h_free[0]])
                    rd.append(tv)
                give(b, rd)
                toks += rd
            return toks

        def x_add(factor=1.0):
            new = [[], []]

            def evac(o, b, h, t):
                xb = X[:, b, 512 * h:512 * h + 512]
                tv = V.do(stt, xb, o, factor, xb, ALU.mult, ALU.add, w=[t, xt[b]])
                new[b].append(tv)
                return [tv]
            return evac, new

        ar = Arena()
        hdep = norm_t("norm_mix_g", 0, Arena(0))

        C = ar([128, 14, S])
        ub = [ar([128, 2, S + 1]) for _ in range(2)]
        dtmp = ar([128, 2, S])
        tz = []
        for i in range(2):
            tz.append(V.do(mset, ub[i][:, :, 0:1], 0.0, w=[hdep]))
        low = ar.here()
        c_tok = {}
        u_free = [None, None]

        def shift_evac(o, c, t):
            i = (c // 256) % 2
            ta = A.do(acopy, ub[i][:, :, 1:S + 1], o, w=[t, tz[i], u_free[i], hdep])
            td = V.do(tt, dtmp[:, :, :], ub[i][:, :, 0:S], ub[i][:, :, 1:S + 1], ALU.subtract, w=[ta])
            for u in range(2):
                n = c // 128 + u
                tv = V.do(stt, C[:, n, :], dtmp[:, u, :], col("rwkv_mu", n), ub[i][:, u, 1:S + 1],
                          ALU.mult, ALU.add, w=[td])
                c_tok[n] = tv
            u_free[i] = tv
            return [ta]

        for c in range(0, 1792, 256):
            proj_t("w_in", 0, c, HH, HL, 256, 8, hdep, shift_evac)

        rT, kT, vT = C[:, 0:4, :], C[:, 4:8, :], C[:, 8:12, :]
        ctall = [c_tok[n] for n in range(14)]
        AR = ar([128, 4, 2, 2, 128])
        BT = ar([128, 4, 2, 128])
        KT = ar([128, 4, 2, 128])
        BON = ar([128, 4, S])
        VN = ar([128, 2, 512])
        keep = ar.here()
        sw = ar([128, 4, S])
        cum = ar([128, 4, 2, 128])
        EP = ar([128, 4, 2, 128])
        aa = ar([128, 4, S])
        sg = C[:, 13, :]
        t12 = A.do(act, C[0:64, 12, :], C[0:64, 12, :], ACT.Tanh, w=[ctall])
        tsg = A.do(act, sg, sg, ACT.Sigmoid, w=[ctall])
        a_tok, w_tok = [], []
        for c2 in range(2):
            bw, fw = take()
            ba, fa = take()
            P.wait(fw, fa, t12, ctall, t_const)
            for u in range(2):
                c = 2 * c2 + u
                o = slice(256 * u, 256 * u + 256)
                w_ = SM("w2a2")[:, 128 * c:128 * c + 128]
                P.do(mm, banks[bw][:, o], w_[0:64, :], C[0:64, 12, :], True, True, inc=False)
                t = P.do(mm, banks[ba][:, o], w_[64:128, :], C[64:128, 12, :], True, True)
            for u in range(2):
                c = 2 * c2 + u
                o = slice(256 * u, 256 * u + 256)
                w_tok.append(A.do(act, sw[:, c, :], banks[bw][:, o], ACT.Sigmoid, bias=col("rwkv_w0", c), w=[t]))
                a_tok.append(A.do(act, aa[:, c, :], banks[ba][:, o], ACT.Sigmoid, bias=col("rwkv_a0", c), w=[t]))
            give(bw, w_tok[-2:])
            give(ba, a_tok[-2:])

        sw4 = sw[:, :, :].rearrange("p c (b n) -> p c b n", b=2)
        ones = K("ones128")
        tcs = []
        for c in range(4):
            for b in range(2):
                tcs.append(V.do(scan, cum[:, c, b, :], ones, sw4[:, c, b, :], 0.0, ALU.mult, ALU.add,
                                w=[w_tok[c], t_const]))
        mid = st[:, 16:24].rearrange("p (c b o) -> p c b o", c=4, b=2)
        tm = V.do(cp, mid, cum[:, :, :, 63:64], w=[tcs])
        tem = A.do(act, st[:, 24:32], st[:, 16:24], ACT.Exp, scale=-GAMMA, w=[tm])
        for c in range(4):
            tcc = V.do(tt, cum[:, c, :, :], cum[:, c, :, :], bc(mid[:, c, :, :], 2, 128), ALU.subtract,
                       w=[tm, tcs])
        V.wait(tcc)
        tep = A.do(act, EP[:, :, :, :], cum[:, :, :, :], ACT.Exp, scale=-GAMMA, w=[tcc])
        r4 = rT.rearrange("p c (b n) -> p c b n", b=2)
        k4 = kT.rearrange("p c (b n) -> p c b n", b=2)
        a4 = aa[:, :, :].rearrange("p c (b n) -> p c b n", b=2)
        for c in range(4):
            trho = V.do(tt, AR[:, c, :, 1, :], r4[:, c, :, :], EP[:, c, :, :], ALU.mult, w=[tep])
        tend = V.do(cp, st[:, 32:36].rearrange("p (c o) -> p c o", o=1), EP[:, :, 0, 127:128], w=[tep])
        tcx = V.do(tt, sw4, cum[:, :, :, :], sw4, ALU.subtract, w=[tcc, tcs])
        kkb = ar([128, 4, S])
        sq = ar([128, 4, S])
        tk = []
        for c in range(4):
            t1 = V.do(ts, kkb[:, c, :], kT[:, c, :], col("rwkv_k_k", c), None, ALU.mult, w=[ctall])
            t2 = A.do(act, sq[:, c, :], kkb[:, c, :], ACT.Square, w=[t1])
            b, fr = take()
            t3 = P.do(mm, banks[b][:, 0:256], K("bones"), sq[:, c, :], True, True, w=[fr, t2])
            t4 = V.do(ts, sq[:, c, :], banks[b][:, 0:256], 1e-24, None, ALU.max, w=[t3])
            give(b, [t4])
            tk.append(t4)
        tl = A.do(act, sq[:, :, :], sq[:, :, :], ACT.Ln, scale=float(2 ** 30), w=[tk])
        tl = A.do(act, sq[:, :, :], sq[:, :, :], ACT.Exp, scale=-0.5, bias=lnsh, w=[tl])
        tkk = V.do(tt, kkb[:, :, :], kkb[:, :, :], sq[:, :, :], ALU.mult, w=[tl])
        txp = A.do(act, EP[:, :, :, :], sw4, ACT.Exp, scale=-GAMMA, w=[tcx, trho, tend])
        kk4 = kkb[:, :, :].rearrange("p c (b n) -> p c b n", b=2)
        for c in range(4):
            talpha = V.do(stt, AR[:, c, :, 0, :], kk4[:, c, :, :], -1.0, EP[:, c, :, :], ALU.mult, ALU.mult,
                          w=[txp, tkk])
        tin = A.do(act, cum[:, :, :, :], cum[:, :, :, :], ACT.Exp, scale=GAMMA, w=[tep, tcx])
        tb = V.do(tt, kkb[:, :, :], kkb[:, :, :], aa[:, :, :], ALU.mult, w=[talpha, a_tok])
        tbeta = V.do(tt, BT[:, :, :, :], kk4, cum[:, :, :, :], ALU.mult, w=[tb, tin])
        for c in range(4):
            t1 = V.do(ts, aa[:, c, :], aa[:, c, :], -1.0, col("rwkv_k_a", c), ALU.add, ALU.mult, w=[tb])
        tk2 = V.do(stt, kT, aa[:, :, :], 1.0, kT, ALU.add, ALU.mult, w=[t1])
        tkap = V.do(tt, KT[:, :, :, :], k4, cum[:, :, :, :], ALU.mult, w=[tk2, tin])
        for c in range(4):
            t1 = V.do(stt, sq[:, c, :], rT[:, c, :], col("rwkv_r_k", c), kT[:, c, :], ALU.mult, ALU.mult,
                      w=[tk2, tkk])
            b, fr = take()
            t2 = P.do(mm, banks[b][:, 0:256], K("bones"), sq[:, c, :], True, True, w=[fr, t1])
            tbon = V.do(tt, BON[:, c, :], banks[b][:, 0:256], vT[:, c, :], ALU.mult, w=[t2])
            give(b, [tbon])
        tvn = []
        for q in range(2):
            b, fr = take()
            P.wait(fr)
            for c in range(4):
                t = P.do(tr, banks[b][:, 128 * c:128 * c + 128], vT[:, c, 128 * q:128 * q + 128], ident,
                         inc=(c == 3))
            tvn.append(A.do(acopy, VN[:, q, :], banks[b][:, :], w=[t]))
            give(b, [tvn[-1]])
        u_start = [tbon, tkap, tbeta, talpha, trho, tin, tvn]
        uar = Arena(keep)
        BKN = uar([128, 2, 512])
        tbk = []
        for n, src in enumerate((BT, KT)):
            b, fr = take()
            P.wait(fr, tbeta, tkap)
            for c in range(4):
                t = P.do(tr, banks[b][:, 128 * c:128 * c + 128], src[:, c, 0, :], ident, inc=(c == 3))
            tbk.append(A.do(acopy, BKN[:, n, :], banks[b][:, :], w=[t, u_start]))
            give(b, [tbk[-1]])
        per = [[uar([128, 4, 128]) for _ in range(5)] for _ in range(2)]
        c_ar = Arena(0)
        d_ar = Arena(14 * 4 * S)
        tmp = [[c_ar([128, 4, 128]) for _ in range(3)] + [d_ar([128, 4, 128]) for _ in range(2 - n)] +
               [uar([128, 4, 128]) for _ in range(2 + n)] for n in range(2)]
        assert d_ar.here() <= low
        US = uar([128, 2, 512])
        SS = uar([128, 4, 64])
        YT = BT[:, :, :, :].rearrange("p c b n -> p c (b n)")
        assert c_ar.here() <= 13 * 4 * S

        def bm(name):
            return bc(K(name).rearrange("p (o n) -> p o n", o=1), 1, 4)

        def b4(i):
            return banks[i][:, :].rearrange("p (u n) -> p u n", u=4)

        t_state = None
        prev = [u_start, u_start]
        ty = []
        for blk in range(2):
            uses = []
            for g in range(2):
                RBT, AKT, RKT, X8, Y1 = per[g]
                T0, T1, T2, T3, T4, T5, T6 = tmp[g]
                sb = []
                b1, f1 = take()
                b2, f2 = take()
                b3, f3 = take()
                b4_, f4 = take()
                b5, f5 = take()
                P.wait(f1, f2, f3, f4, f5, u_start)
                for i in range(4):
                    c, p0 = i, 64 * g
                    al = AR[p0:p0 + 64, c, blk, 0, :]
                    rh = AR[p0:p0 + 64, c, blk, 1, :]
                    be = BT[p0:p0 + 64, c, blk, :]
                    ka = KT[p0:p0 + 64, c, blk, :]
                    for bb, l, r in ((b1, be, al), (b2, al, be), (b3, be, rh), (b4_, ka, al), (b5, ka, rh)):
                        t = P.do(mm, banks[bb][:, 128 * i:128 * i + 128], l, r, True, True, inc=(i == 3))
                        if i == 3:
                            sb.append(t)
                pv = prev[g]
                dT = V.do(tt, T0[:, :, :], b4(b1), bm("dgt"), ALU.mult, w=[sb[0], pv])
                dN = V.do(tt, T1[:, :, :], b4(b2), bm("dgn"), ALU.mult, w=[sb[1], pv])
                lN = V.do(tt, T2[:, :, :], b4(b2), bm("ofn"), ALU.mult, w=[sb[1], pv])
                give(b1, [dT])
                give(b2, [dN, lN])
                rb = V.do(tt, RBT[:, :, :], b4(b3), bm("incl"), ALU.mult, w=[sb[2], pv])
                ak = V.do(tt, AKT[:, :, :], b4(b4_), bm("strict"), ALU.mult, w=[sb[3], pv])
                rk = V.do(tt, RKT[:, :, :], b4(b5), bm("incl"), ALU.mult, w=[sb[4], pv])
                give(b3, [rb])
                give(b4_, [ak])
                give(b5, [rk])
                x1 = V.do(tt, T5[:, :, :], T0[:, :, :], bm("ident"), ALU.add, w=[dT, pv])

                def prod(l, r, deps):
                    b, fr = take()
                    P.wait(fr, *deps)
                    for i in range(4):
                        t = P.do(mm, banks[b][:, 128 * i:128 * i + 128], l[:, i, :], r[:, i, :], True, True,
                                 inc=(i == 3))
                    return b, t

                def to(eng, dst, bt, extra=None, more=()):
                    b, t = bt
                    if extra is not None:
                        k = V.do(tt, dst[:, :, :], b4(b), extra, ALU.add, w=[t, *more])
                    elif eng is A:
                        k = A.do(acopy, dst[:, :, :], b4(b), w=[t, *more])
                    else:
                        k = V.do(cp, dst[:, :, :], b4(b), w=[t, *more])
                    give(b, [k])
                    return k

                p1 = prod(T0, T1, [dT, dN])
                p2 = prod(T1, T0, [dT, dN])
                d2 = to(A, T3, p1)
                d2t = to(A, T4, p2)
                p3 = prod(T3, T5, [d2, x1])
                p4 = prod(T4, T3, [d2t])
                p5 = prod(T3, T4, [d2t])
                x2 = to(V, T0, p3, T5[:, :, :], [x1, p1[1], p2[1]])
                d4 = to(A, T1, p4, more=[p2[1]])
                d4t = to(A, T6, p5)
                p6 = prod(T1, T0, [d4, x2])
                p7 = prod(T6, T1, [d4t])
                x4 = to(V, T5, p6, T0[:, :, :], [p3[1]])
                d8 = to(A, T3, p7, more=[p5[1]])
                p8 = prod(T3, T5, [d8, x4])
                x8 = to(V, X8, p8, T5[:, :, :], [x4])
                p9 = prod(X8, T2, [x8, lN])
                p10 = prod(T2, X8, [x8, lN])
                n1 = to(A, T0, p9, more=[p6[1], x4])
                n1t = to(A, T1, p10, more=[p7[1]])
                p11 = prod(T1, T0, [n1, n1t])
                p12 = prod(T0, T1, [n1, n1t])
                n2 = to(A, T3, p11, more=[p8[1]])
                n2t = to(A, T4, p12, more=[p5[1]])
                p13 = prod(T3, T4, [n2, n2t])
                y4 = to(V, T5, p13, bm("ident"), [p8[1], x8])
                p14 = prod(T3, T5, [y4])
                y2 = to(V, T6, p14, T5[:, :, :], [y4, p7[1]])
                p15 = prod(T0, T6, [y2])
                y1 = to(V, Y1, p15, T6[:, :, :], [y2])
                uses.append((rb, ak, rk, x8, y1))
            def heads(k, g):
                return US[:, k, :].rearrange("p (i g d) -> p g i d", g=2, d=64)[:, g, :, :]

            def step(k, dst, first):
                tk = []
                for g in range(2):
                    b, fr = take()
                    P.wait(fr, tvn if first else tu)
                    for i in range(4):
                        h = 2 * i + g
                        P.wait(uses[g][k[1]])
                        o = banks[b][:, 64 * i:64 * i + 64]
                        if first:
                            t = P.do(mm, o, per[g][k[0]][:, i, :], VN[:, blk, 64 * h:64 * h + 64], True, blk == 0)
                            if blk == 1:
                                P.wait(t_state)
                                t = P.do(mm, o, AR[64 * g:64 * g + 64, i, 1, 0, :], SS[64 * g:64 * g + 64, i, :],
                                         False, True)
                        else:
                            t = P.do(mm, o, per[g][k[0]][:, i, :], US[:, 1 - dst, 64 * h:64 * h + 64], True, True)
                    k_ = A.do(acopy, heads(dst, g), banks[b][:, 0:256].rearrange("p (i d) -> p i d", i=4),
                              w=[t, ty])
                    give(b, [k_])
                    tk.append(k_)
                return tk

            tu = None
            tu = step((1, 1), 1, True)
            tu = step((3, 3), 0, False)
            tu = step((4, 4), 1, False)
            b, fr = take()
            P.wait(fr, tu)
            for h in range(8):
                g, i = h % 2, h // 2
                P.wait(uses[g][0], uses[g][2])
                p0 = 64 * (h % 2)
                o = banks[b][p0:p0 + 64, 128 * (h // 2):128 * (h // 2) + 128]
                P.do(mm, o, US[:, 1, 64 * h:64 * h + 64], per[g][0][:, i, :], True, False, inc=False)
                t = P.do(mm, o, VN[:, blk, 64 * h:64 * h + 64], per[g][2][:, i, :], False, blk == 0)
                if blk == 1:
                    t = P.do(mm, o, SS[p0:p0 + 64, h // 2, :], AR[p0:p0 + 64, h // 2, 1, 1, :], False, True)
            y = A.do(acopy, YT[:, :, 128 * blk:128 * blk + 128], b4(b), w=[t])
            give(b, [y])
            ty.append(y)
            if blk == 0:
                b, fr = take()
                P.wait(fr, tbk)
                for h in range(8):
                    p0 = 64 * (h % 2)
                    o = banks[b][p0:p0 + 64, 64 * (h // 2):64 * (h // 2) + 64]
                    P.do(mm, o, BKN[:, 0, 64 * h:64 * h + 64], US[:, 1, 64 * h:64 * h + 64], True, False, inc=False)
                    t = P.do(mm, o, BKN[:, 1, 64 * h:64 * h + 64], VN[:, 0, 64 * h:64 * h + 64], False, True)
                t_state = []
                for c in range(4):
                    t_state.append(V.do(ts, SS[:, c, :], banks[b][:, 64 * c:64 * c + 64], st[:, 32 + c:33 + c],
                                        st[:, 24 + 2 * c + 1:24 + 2 * c + 2], ALU.mult, ALU.mult,
                                        w=[t, tem, tend]))
                give(b, t_state)
                prev = [[t], [t]]
        far = Arena(keep)
        m1 = far([128, 4, S])
        m2 = far([128, 4, S])
        assert far.here() <= keep + 4 * (2 * 512 + 10 * 512)
        oaH = Arena(0)([128, 4, S], R)
        oaL = Arena(4 * 1024)([128, 4, S], R)
        oa_tok = []
        for c in range(4):
            ta = A.do(act, m2[:, c, :], YT[:, c, :], ACT.Square, w=[ty, t])
            b, fr = take()
            P.do(mm, banks[b][:, 0:256], K("bones"), YT[:, c, :], True, True, w=[fr, ty], inc=False)
            t1 = P.do(mm, banks[b][:, 256:512], K("bones"), m2[:, c, :], True, True, w=[ta])
            t2 = V.do(ts, m1[:, c, :], banks[b][:, 0:256], 1.0 / 64, None, ALU.mult, w=[t1, t])
            t3 = V.do(tt, m2[:, c, :], m1[:, c, :], m1[:, c, :], ALU.mult, w=[t2])
            t4 = V.do(stt, m2[:, c, :], banks[b][:, 256:512], 1.0 / 64, m2[:, c, :], ALU.mult, ALU.subtract,
                      w=[t3])
            give(b, [t4])
            t4 = V.do(ts, m2[:, c, :], m2[:, c, :], 0.0, None, ALU.max, w=[t4])
            t5 = V.do(tt, m1[:, c, :], YT[:, c, :], m1[:, c, :], ALU.subtract, w=[t3])
            t6 = A.do(act, m2[:, c, :], m2[:, c, :], ACT.Ln, bias=epsgn, w=[t4])
            t6 = A.do(act, m2[:, c, :], m2[:, c, :], ACT.Exp, scale=-0.5, w=[t6])
            t7 = V.do(tt, m1[:, c, :], m1[:, c, :], m2[:, c, :], ALU.mult, w=[t5, t6])
            t8 = V.do(ts, m1[:, c, :], m1[:, c, :], col("rwkv_lnx_w", c), col("rwkv_lnx_b", c), ALU.mult, ALU.add,
                      w=[t7])
            t9 = V.do(tt, m1[:, c, :], m1[:, c, :], BON[:, c, :], ALU.add, w=[t8, tbon])
            b, fr = take()
            t1 = P.do(mm, banks[b][:, 0:256], SM("g2")[:, 128 * c:128 * c + 128], sg, True, True, w=[fr, tsg])
            t10 = V.do(tt, m1[:, c, :], m1[:, c, :], banks[b][:, 0:256], ALU.mult, w=[t9, t1])
            give(b, [t10])
            th = A.do(acopy, oaH[:, c, :], m1[:, c, :], w=[t10, t])
            tl_ = V.do(tt, oaL[:, c, :], m1[:, c, :], oaH[:, c, :].bitcast(F), ALU.subtract, w=[th, t])
            oa_tok += [th, tl_]

        dar = Arena(8 * 1024)
        obH = dar([128, 4, S], R)
        obL = dar([128, 4, S], R)
        qT = dar([128, 4, S])
        kTt = dar([128, 4, S])
        vN = dar([128, 2, 512])
        base_dep = oa_tok
        q_tok, k_tok, v_tok = [], [], []

        def diff_evac(o, c, t):
            n = (c - 1792) // 128
            if n < 4:
                k = A.do(act, qT[:, n:n + 2, :], o, ACT.Copy, scale=0.125, w=[t, base_dep])
                q_tok.append(k)
            else:
                k = V.do(cp, kTt[:, n - 4:n - 2, :], o, w=[t, base_dep])
                k_tok.append(k)
            return [k]

        for c in range(1792, 2816, 256):
            proj_t("w_in", 0, c, HH, HL, 256, 8, hdep, diff_evac)

        def v_evac(o, b, h, t):
            k = A.do(acopy, vN[:, b, :], o, w=[t, base_dep])
            v_tok.append(k)
            return [k]

        proj_n("w_in", 0, 8, 2816, 512, HH, HL, hdep, v_evac)

        lamv = st[:, 40:48]
        lj = dar([128, 64])
        tl1 = V.do(ttr, lj[:, :], SM("lam")[:, 0:64], SM("lam")[:, 64:128], ALU.mult, ALU.add, 0.0, st[:, 40:41],
                   w=[t_const, base_dep])
        tl2 = V.do(ttr, lj[:, :], SM("lam")[:, 128:192], SM("lam")[:, 192:256], ALU.mult, ALU.add, 0.0,
                   st[:, 41:42], w=[tl1])
        tl3 = A.do(act, st[:, 42:44], st[:, 40:42], ACT.Exp, w=[tl1, tl2])
        tl4 = V.do(tt, st[:, 44:45], st[:, 42:43], st[:, 43:44], ALU.subtract, w=[tl3])
        t_nlam = V.do(ts, st[:, 45:46], st[:, 44:45], 0.2, -1.0, ALU.add, ALU.mult, w=[tl4])

        def soft(qa, ka, bias, E, sc, deps, e_free):
            b, fr = take()
            P.wait(fr, *deps)
            P.do(mm, banks[b][:, 0:128], qa[:, 0:128], ka[:, 0:128], True, True, inc=False)
            t = P.do(mm, banks[b][:, 128:384], qa[:, 128:256], ka[:, 0:256], True, True)
            r0 = V.do(ttr, E[:, 0:128], banks[b][:, 0:128], bias[:, 0:128], ALU.add, ALU.max, -3.0e38,
                      sc[:, 0:1], w=[t, e_free])
            r1 = V.do(ttr, E[:, 128:384], banks[b][:, 128:384], bias[:, 128:384], ALU.add, ALU.max, -3.0e38,
                      sc[:, 1:2], w=[t, e_free])
            give(b, [r0, r1])
            nm = V.do(ts, sc[:, 2:4], sc[:, 0:2], -1.0, None, ALU.mult, w=[r0, r1])
            e0 = A.do(act, E[:, 0:128], E[:, 0:128], ACT.Exp, bias=sc[:, 2:3], accum_out=sc[:, 4:5], w=[nm])
            e1 = A.do(act, E[:, 128:384], E[:, 128:384], ACT.Exp, bias=sc[:, 3:4], accum_out=sc[:, 5:6], w=[nm])
            return V.do(rcp, sc[:, 6:8], sc[:, 4:6], w=[e0, e1])

        def turn(E, ET, deps, et_free):
            b, fr = take()
            P.wait(fr, *deps)
            for i in range(3):
                t = P.do(tr, banks[b][:, 128 * i:128 * i + 128], E[:, 128 * i:128 * i + 128], ident, inc=(i == 2))
            k = A.do(acopy, ET[:, :], banks[b][:, 0:384], w=[t, et_free])
            give(b, [k])
            return t, k

        def pv(o, v0, v1, ET):
            P.do(mm, o, v0, ET[:, 0:256], True, False, inc=False)
            return P.do(mm, o[:, 128:256], v1, ET[:, 256:384], False, True)

        Es = [dar([128, 384]) for _ in range(4)]
        ETs = [dar([128, 384]) for _ in range(2)]
        oT = [dar([128, S]) for _ in range(2)]
        sqd = [dar([128, S]) for _ in range(2)]
        AB = dar([128, 4, 384])
        tab_ = [V.do(stt, AB[:, h, :], K("ndist"), 2.0 ** (-2.0 * (h + 1)), K("caus"), ALU.mult, ALU.add,
                     w=[t_const, base_dep]) for h in range(4)]
        ef, etf, of = [None] * 4, [None] * 2, [None] * 2
        ob_tok = []
        for h in range(4):
            bias = AB[:, h, :]
            i0 = 2 * (h % 2)
            scs = [st[:, 48 + 8 * (i0 + c):56 + 8 * (i0 + c)] for c in range(2)]
            rr = []
            for c in range(2):
                rr.append(soft(qT[64 * c:64 * c + 64, h, :], kTt[64 * c:64 * c + 64, h, :], bias, Es[i0 + c],
                               scs[c], [q_tok, k_tok], [ef[i0 + c], base_dep, tab_]))
            tn = V.do(ts, scs[1][:, 6:8], scs[1][:, 6:8], st[:, 45:46], None, ALU.mult, w=[rr[1], t_nlam])
            w_ = []
            for m, (a, z) in enumerate(((0, 128), (128, 384))):
                t1 = V.do(ts, Es[i0 + 1][:, a:z], Es[i0 + 1][:, a:z], scs[1][:, 6 + m:7 + m], None, ALU.mult,
                          w=[tn])
                w_.append(V.do(stt, Es[i0][:, a:z], Es[i0][:, a:z], scs[0][:, 6 + m:7 + m], Es[i0 + 1][:, a:z],
                               ALU.mult, ALU.add, w=[t1, rr[0]]))
            j = h % 2
            tE, tET = turn(Es[i0], ETs[j], [w_], [etf[j], base_dep])
            ef[i0] = ef[i0 + 1] = tE
            b, fr = take()
            P.wait(fr, tET, v_tok)
            t = pv(banks[b][:, 0:256], vN[:, 0, 128 * h:128 * h + 128], vN[:, 1, 128 * h:128 * h + 128], ETs[j])
            etf[j] = t
            t1 = V.do(cp, oT[j][:, :], banks[b][:, 0:256], w=[t, of[j], base_dep])
            t2 = A.do(act, sqd[j][:, :], banks[b][:, 0:256], ACT.Square, w=[t1, of[j], base_dep])
            give(b, [t1, t2])
            b, fr = take()
            t3 = P.do(mm, banks[b][:, 0:256], K("ones128"), sqd[j][:, :], True, True, w=[fr, t2])
            t4 = A.do(act, sqd[j][:, :], banks[b][:, 0:256], ACT.Ln, scale=1.0 / 128, bias=epssub, w=[t3])
            give(b, [t4])
            t5 = A.do(act, sqd[j][:, :], sqd[j][:, :], ACT.Exp, scale=-0.5, w=[t4])
            t6 = V.do(tt, oT[j][:, :], oT[j][:, :], sqd[j][:, :], ALU.mult, w=[t1, t5])
            t7 = V.do(ts, oT[j][:, :], oT[j][:, :], col("diff_subln_g"), 0.8, ALU.mult, ALU.mult, w=[t6])
            th = A.do(acopy, obH[:, h, :], oT[j][:, :], w=[t7, base_dep])
            tl_ = V.do(tt, obL[:, h, :], oT[j][:, :], obH[:, h, :].bitcast(F), ALU.subtract, w=[th])
            of[j] = tl_
            ob_tok += [th, tl_]

        gar = Arena(16 * 1024)
        gT = gar([128, 16, S])
        mH = gar([128, 8, S], R)
        mL = gar([128, 8, S], R)
        mt = gar([128, 8, S])
        g_tok = []

        def gate_evac(o, c, t):
            n = (c - 3328) // 128
            k = A.do(act, gT[:, n:n + 2, :], o, ACT.Sigmoid, w=[t, ob_tok])
            g_tok.append(k)
            return [k]

        for c in range(3328, 5376, 256):
            proj_t("w_in", 0, c, HH, HL, 256, 8, hdep, gate_evac)
        h_free[0] = (P.sem, P.n)
        ma = {}

        def pa_evac(o, c, t):
            n = c // 128
            ma[n] = V.do(tt, mt[:, n:n + 2, :], o, gT[:, n:n + 2, :], ALU.mult, w=[t, g_tok])
            return [ma[n]]

        for c in range(0, 1024, 512):
            proj_t("w_proj_a", 0, c, oaH, oaL, 512, 4, oa_tok, pa_evac)
        m_tok = []

        def pb_evac(o, c, t):
            n = c // 128
            t1 = V.do(tt, gT[:, 8 + n:10 + n, :], o, gT[:, 8 + n:10 + n, :], ALU.mult, w=[t, g_tok])
            t2 = V.do(tt, mt[:, n:n + 2, :], mt[:, n:n + 2, :], gT[:, 8 + n:10 + n, :], ALU.add, w=[t1, ma[n]])
            t3 = A.do(acopy, mH[:, n:n + 2, :], mt[:, n:n + 2, :], w=[t2])
            t4 = V.do(tt, mL[:, n:n + 2, :], mt[:, n:n + 2, :], mH[:, n:n + 2, :].bitcast(F), ALU.subtract,
                      w=[t3])
            m_tok.extend([t3, t4])
            return [t1]

        for c in range(0, 1024, 512):
            proj_t("w_proj_b", 0, c, obH, obL, 512, 4, ob_tok, pb_evac)
        ev, new = x_add()
        proj_n("w_out", 0, 8, 0, 1024, mH, mL, m_tok, ev)
        xt[0], xt[1] = new

        def ff_bufs(n):
            a = Arena(0)
            return a([128, n, S], R), a([128, n, S], R), a

        def last_pe():
            return (P.sem, P.n)

        hdep = norm_t("norm_mlp_g", 0, Arena(0))
        sH, sL, fa = ff_bufs(32)
        rl = [fa([128, 2, S]) for _ in range(2)]
        f_tok = []
        rf = [None, None]
        prevd = [hdep, last_pe()]

        def relu_evac(o, c, t):
            n = c // 128
            j = (n // 2) % 2
            t1 = V.do(ts, rl[j][:, :, :], o, 0.0, None, ALU.max, w=[t, rf[j], prevd])
            t2 = A.do(act, sH[:, n:n + 2, :], rl[j][:, :, :], ACT.Square, w=[t1, prevd])
            t3 = V.do(tt, rl[j][:, :, :], rl[j][:, :, :], rl[j][:, :, :], ALU.mult, w=[t2])
            t4 = V.do(tt, sL[:, n:n + 2, :], rl[j][:, :, :], sH[:, n:n + 2, :].bitcast(F), ALU.subtract, w=[t3])
            rf[j] = t4
            f_tok.extend([t2, t4])
            return [t1]

        for c in range(0, 4096, 256):
            proj_t("w_ff1", 0, c, HH, HL, 256, 8, hdep, relu_evac)
        h_free[0] = last_pe()
        ev, new = x_add()
        proj_n("w_ff2", 0, 32, 0, 1024, sH, sL, f_tok, ev)
        xt[0], xt[1] = new

        pe_done = last_pe()
        V.wait(pe_done)
        A.wait(pe_done)
        hdep = norm_t("norm_ple_g", 0, Arena(0))
        par = Arena(8 * 1024)
        pr = par([128, 2, S])
        pH = par([128, 2, S], R)
        pL = par([128, 2, S], R)
        sgt = par([128, 2, D])
        frow = par([128, D])
        s_p = sem("s_p")
        SP.dma(pr[:, :, :], pin, s_p, w=[pe_done])
        SP.dma(frow[:, :], rowin, s_row, w=[pe_done])
        th = A.do(acopy, pH[:, :, :], pr[:, :, :], w=[(s_p, 16)])
        tl_ = V.do(tt, pL[:, :, :], pr[:, :, :], pH[:, :, :].bitcast(F), ALU.subtract, w=[th])
        sgtok = {}

        def sg_evac(o, b, h, t):
            k = A.do(act, sgt[:, b, 512 * h:512 * h + 512], o, ACT.Sigmoid, w=[t])
            sgtok[b, h] = k
            return [k]

        proj_n("w_ple_gate", 0, 8, 0, 1024, HH, HL, hdep, sg_evac)
        h_free[0] = last_pe()
        new = [[], []]

        def ple_evac(o, b, h, t):
            g = sgt[:, b, 512 * h:512 * h + 512]
            xb = X[:, b, 512 * h:512 * h + 512]
            t1 = V.do(tt, g, o, g, ALU.mult, w=[t, sgtok[b, h]])
            t2 = V.do(tt, xb, xb, g, ALU.add, w=[t1, xt[b]])
            new[b].append(t2)
            return [t1]

        proj_n("w_ple", 0, 2, 0, 1024, pH, pL, [th, tl_], ple_evac)
        xt[0], xt[1] = new
        nsc = Arena(0)([128, 2, D])
        tr_ = rms_stat(xt, nsc)
        for b in range(2):
            t = V.do(stt, X[:, b, :], X[:, b, :], st[:, 4 + b:5 + b], frow[:, :], ALU.mult, ALU.mult,
                     w=[tr_, (s_row, 16)])
            xt[b] = [t]

        def swiglu(n, layer):
            nonlocal hdep
            d0 = last_pe()
            V.wait(d0)
            A.wait(d0)
            hdep = norm_t(f"norm_ffn{n}_2", 8 * layer, Arena(0))
            d1 = list(hdep)
            aH, aL, fa_ = ff_bufs(22)
            sgm = [fa_([128, 2, S]) for _ in range(2)]
            gfr = [None, None]
            toks = []
            held = {}

            def g_evac(o, c, t):
                j = (c // 256) % 2
                t1 = A.do(act, sgm[j][:, :, :], o, ACT.Sigmoid, w=[t, gfr[j], d1])
                t2 = V.do(tt, sgm[j][:, :, :], o, sgm[j][:, :, :], ALU.mult, w=[t1])
                held[c] = t2
                return [t1, t2]

            def u_evac(o, c, t):
                j = (c // 256) % 2
                m = c // 128
                t1 = V.do(tt, sgm[j][:, :, :], o, sgm[j][:, :, :], ALU.mult, w=[t, held[c]])
                t2 = A.do(acopy, aH[:, m:m + 2, :], sgm[j][:, :, :], w=[t1, d1])
                t3 = V.do(tt, aL[:, m:m + 2, :], sgm[j][:, :, :], aH[:, m:m + 2, :].bitcast(F), ALU.subtract,
                          w=[t2, d1])
                gfr[j] = t3
                toks.extend([t2, t3])
                return [t1]

            for c in range(0, 2816, 256):
                proj_t(f"ffn{n}_w_gate_2", layer, c, HH, HL, 256, 8, hdep, g_evac)
                proj_t(f"ffn{n}_w_up_2", layer, c, HH, HL, 256, 8, hdep, u_evac)
            h_free[0] = last_pe()
            e_, new_ = x_add(0.5)
            proj_n(f"ffn{n}_w_down_2", layer, 22, 0, 1024, aH, aL, toks, e_)
            xt[0], xt[1] = new_

        def qk_norm(o, b, t, g, gs, dst, dtok, w8, scale, deps, wfree):
            sqb, qn, q2 = w8
            r3 = o.rearrange("p (h d) -> p h d", h=8)
            q3 = qn[:, :].rearrange("p (h d) -> p h d", h=8)
            z3 = q2[:, :].rearrange("p (h d) -> p h d", h=8)
            s3 = sqb[:, :].rearrange("p (h d) -> p h d", h=8)
            ss, sr = st[:, 96:104], st[:, 104:112]
            t1 = A.do(act, sqb[:, :], o, ACT.Square, w=[t, wfree, deps])
            t2 = V.do(red, ss, s3, ALU.add, w=[t1])
            t3 = A.do(act, sr, ss, ACT.Ln, scale=1.0 / 64, bias=eps6, w=[t2])
            t3 = A.do(act, sr, sr, ACT.Exp, scale=-0.5, w=[t3])
            t4 = V.do(tt, q3, r3, bc(sr.rearrange("p (h o) -> p h o", o=1), 2, 64), ALU.mult,
                      w=[t3, wfree, deps])

            def tab(x):
                return bc(x.rearrange("p (o d) -> p o d", o=1), 1, 8)
            if gs is None:
                t5 = V.do(tt, q3, q3, tab(g), ALU.mult, w=[t4])
            else:
                t6 = V.do(tt, z3[:, :, 0:32], q3[:, :, 32:64], tab(gs[:, 0:32]), ALU.mult, w=[t4])
                t7 = V.do(tt, z3[:, :, 32:64], q3[:, :, 0:32], tab(gs[:, 32:64]), ALU.mult, w=[t4])
                t8 = V.do(tt, q3, q3, tab(g), ALU.mult, w=[t6, t7])
                t5 = V.do(tt, q3, q3, z3, ALU.add, w=[t8])
            bb, fr = take()
            P.wait(fr, t5)
            for c in range(4):
                tp = P.do(tr, banks[bb][:, 128 * c:128 * c + 128], qn[:, 128 * c:128 * c + 128], ident,
                          inc=(c == 3))
            k = A.do(act, dst[:, :, 128 * b:128 * b + 128], b4(bb), ACT.Copy, scale=scale, w=[tp, deps])
            give(bb, [k])
            dtok.append(k)
            return [t1, t4], tp

        def rope_tabs(ar_, gname, gsname, deps):
            g = ar_([128, 2, 64])
            gs = ar_([128, 2, 64])
            c_ = K("cos").rearrange("p (b d) -> p b d", b=2)
            s_ = K("sin").rearrange("p (b d) -> p b d", b=2)
            for b in range(2):
                V.do(tt, g[:, b, :], c_[:, b, :], SM(gname), ALU.mult, w=deps)
                t = V.do(tt, gs[:, b, :], s_[:, b, :], SM(gsname), ALU.mult)
            return g, gs, t

        def attention(layer):
            nonlocal hdep
            d0 = last_pe()
            V.wait(d0)
            A.wait(d0)
            hdep = norm_t("norm_mix_2", 8 * layer, Arena(0))
            a_ = Arena(0)
            mH_ = a_([128, 8, S], R)
            mL_ = a_([128, 8, S], R)
            Q = a_([128, 8, S])
            KK = a_([128, 8, S])
            VV = a_([128, 2, D])
            w8 = [[a_([128, 512]) for _ in range(3)] for _ in range(1)]
            fl = a_.here()
            qtok, ktok, vtok = [], [], []
            wf = [None]
            jj = [0]
            if layer == 0:
                def a_evac(dst, tk, c0, scale):
                    def f(o, c, t):
                        n = (c - c0) // 128
                        k = A.do(act, dst[:, n:n + 2, :], o, ACT.Copy, scale=scale, w=[t, hdep])
                        tk.append(k)
                        return [k]
                    return f
                f1, f2 = a_evac(Q, qtok, 0, 0.125), a_evac(KK, ktok, 1024, 1.0)
                for c in range(0, 512, 256):
                    proj_t("w_in_ab_2", 0, c, HH, HL, 256, 8, hdep, f1)
                for c in range(1024, 1536, 256):
                    proj_t("w_in_ab_2", 0, c, HH, HL, 256, 8, hdep, f2)
                gq, gqs, tg = rope_tabs(a_, "gq", "gqs", hdep)
                gk, gks, tg2 = rope_tabs(a_, "gk", "gks", hdep)
                jobs = [(512, Q, qtok, gq, gqs, 0.125, 4), (1536, KK, ktok, gk, gks, 1.0, 4)]
                wn = "w_in_ab_2"
            else:
                gq, gqs, tg = rope_tabs(a_, "gqd", "gqds", hdep)
                gk, gks, tg2 = rope_tabs(a_, "gkd", "gkds", hdep)
                jobs = [(0, Q, qtok, None, None, 0.125, 0), (512, Q, qtok, gq, gqs, 0.125, 4),
                        (1024, KK, ktok, None, None, 1.0, 0), (1536, KK, ktok, gk, gks, 1.0, 4)]
                wn = "w_in_cd_2"
            for c, dst, tk, g, gs, scale, n0 in jobs:
                def q_evac(o, b, h, t):
                    ga = SM("gqc") if g is None and dst is Q else SM("gkc") if g is None else g[:, b, :]
                    rd, tp = qk_norm(o, b, t, ga, None if gs is None else gs[:, b, :], dst[:, n0:n0 + 4, :], tk,
                                     w8[0], scale, [hdep, tg, tg2], wf[0])
                    wf[0] = tp
                    return rd
                proj_n(wn, 0, 8, c, 512, HH, HL, hdep, q_evac)

            def vv_evac(o, b, h, t):
                k = A.do(acopy, VV[:, b, 512 * h:512 * h + 512], o, w=[t, hdep])
                vtok.append(k)
                return [k]

            proj_n(wn, 0, 8, 2048, 1024, HH, HL, hdep, vv_evac)
            ctok = []
            if layer == 1:
                wfh = a_([128, 64], R)
                wfl = a_([128, 64], R)
                cf = a_([8, 2, S])
                f1 = A.do(acopy, wfh[:, :], SM("wf"), w=[hdep])
                f2 = V.do(tt, wfl[:, :], SM("wf"), wfh[:, :].bitcast(F), ALU.subtract, w=[f1])
                b, fr = take()
                P.wait(fr, f1, f2, hdep)
                o = banks[b][0:8, 0:256]
                for k in range(8):
                    t = mm3(o, wfh[:, 8 * k:8 * k + 8], wfl[:, 8 * k:8 * k + 8], HH[:, k, :], HL[:, k, :],
                            k == 0, k == 7)
                z, e = cf[:, 0, :], cf[:, 1, :]
                t1 = V.do(ts, z, o, SM("bf", 0, 8), None, ALU.add, w=[t])
                give(b, [t1])
                t2 = A.do(act, e, z, ACT.Abs, w=[t1])
                t3 = A.do(act, e, e, ACT.Exp, scale=-1.0, w=[t2])
                t3 = A.do(act, e, e, ACT.Ln, bias=one1[0:8, :], w=[t3])
                t4 = V.do(stt, z, z, 0.0, e, ALU.min, ALU.subtract, w=[t3])
                t5 = V.do(scan, e, bc(K("ones128", 8)[:, 0:1], 1, 256), z, 0.0, ALU.mult, ALU.add, w=[t4])
                t6 = V.do(ts, z, e, -1.0, None, ALU.mult, w=[t5])
                ctok = [t5, t6]
            h_free[0] = last_pe()
            Eb = [a_([128, 384]) for _ in range(3)]
            ETb = [a_([128, 384]) for _ in range(2)]
            ef_, etf_ = [None] * 3, [None] * 2
            mtok = []

            def o_evac(h, b, t):
                m = h // 2
                k1 = A.do(acopy, mH_[:, m, :], banks[b][:, 0:256], w=[t, hdep])
                k2 = V.do(tt, mL_[:, m, :], banks[b][:, 0:256], mH_[:, m, :].bitcast(F), ALU.subtract, w=[k1])
                give(b, [k1, k2])
                mtok.extend([k1, k2])

            n_ = 0
            ob = None
            for h in range(16):
                m, p0 = h // 2, 64 * (h % 2)
                qa, ka = Q[p0:p0 + 64, m, :], KK[p0:p0 + 64, m, :]
                i, j = h % 3, h % 2
                if h % 2 == 0:
                    ob = take()
                    P.wait(ob[1])
                if layer == 0 and h < 8:
                    b, fr = take()
                    b2, fr2 = take()
                    P.wait(fr, fr2, qtok, ktok)
                    P.do(mm, banks[b][:, 0:256], ka[:, 0:128], qa[:, 0:256], True, True, inc=False)
                    t = P.do(mm, banks[b][:, 256:384], ka[:, 128:256], qa[:, 128:256], True, True)
                    z = banks[b][:, 0:384]
                    t1 = A.do(act, Eb[i][:, :], z, ACT.Abs, w=[t, ef_[i]])
                    t2 = A.do(act, Eb[i][:, :], Eb[i][:, :], ACT.Exp, scale=-1.0, w=[t1])
                    t2 = A.do(act, Eb[i][:, :], Eb[i][:, :], ACT.Ln, bias=one1, w=[t2])
                    t3 = V.do(stt, Eb[i][:, :], z, 0.0, Eb[i][:, :], ALU.max, ALU.add, w=[t2])
                    t4 = V.do(tt, Eb[i][:, 0:128], Eb[i][:, 0:128], K("strict"), ALU.mult, w=[t3])
                    t5 = V.do(tt, Eb[i][:, 256:384], Eb[i][:, 256:384], K("strict"), ALU.mult, w=[t3])
                    give(b, [t1, t3])
                    P.do(mm, banks[b2][:, 0:256], ka[:, 0:128], qa[:, 0:256], True, False, inc=False)
                    P.do(mm, banks[b2][:, 0:256], K("ntri"), Eb[i][:, 0:256], False, False, w=[t4, t5], inc=False)
                    P.do(mm, banks[b2][:, 128:256], K("nones"), Eb[i][:, 256:384], False, True, inc=False)
                    P.do(mm, banks[b2][:, 256:384], ka[:, 128:256], qa[:, 128:256], True, False, inc=False)
                    t6 = P.do(mm, banks[b2][:, 256:384], K("ntri"), Eb[i][:, 256:384], False, True)
                    ef_[i] = t6
                    t7 = A.do(act, ETb[j][:, :], banks[b2][:, 0:384], ACT.Exp, w=[t6, etf_[j]])
                    give(b2, [t7])
                    t8 = V.do(tt, ETb[j][:, 0:128], ETb[j][:, 0:128], K("strict"), ALU.mult, w=[t7])
                    t9 = V.do(tt, ETb[j][:, 256:384], ETb[j][:, 256:384], K("strict"), ALU.mult, w=[t7])
                    et = [t7, t8, t9]
                else:
                    bias = K("dil") if (layer == 1 and h >= 8) else K("caus")
                    sc = st[:, 48 + 8 * i:56 + 8 * i]
                    if layer == 1 and h < 8:
                        b, fr = take()
                        P.wait(fr, qtok, ktok, ctok)
                        selh = bc(K("ident", 8)[:, h:h + 1], 1, 128)
                        c_, nc_ = cf[:, 1, :], cf[:, 0, :]
                        for q, (a0, a1) in enumerate(((0, 128), (128, 384))):
                            w_ = a1 - a0
                            o = banks[b][:, a0:a1]
                            P.do(mm, o, qa[:, 128 * q:128 * q + 128], ka[:, 0:w_], True, False, inc=False)
                            P.do(mm, o, selh, nc_[:, 0:w_], False, False, inc=False)
                            for u in range(w_ // 128):
                                t = P.do(mm, o[:, 128 * u:128 * u + 128], c_[:, 128 * q:128 * q + 128], selh,
                                         False, u == w_ // 128 - 1)
                        E = Eb[i]
                        r0 = V.do(ttr, E[:, 0:128], banks[b][:, 0:128], bias[:, 0:128], ALU.add, ALU.max,
                                  -3.0e38, sc[:, 0:1], w=[t, ef_[i]])
                        r1 = V.do(ttr, E[:, 128:384], banks[b][:, 128:384], bias[:, 128:384], ALU.add, ALU.max,
                                  -3.0e38, sc[:, 1:2], w=[t, ef_[i]])
                        give(b, [r0, r1])
                        nm = V.do(ts, sc[:, 2:4], sc[:, 0:2], -1.0, None, ALU.mult, w=[r0, r1])
                        e0 = A.do(act, E[:, 0:128], E[:, 0:128], ACT.Exp, bias=sc[:, 2:3],
                                  accum_out=sc[:, 4:5], w=[nm])
                        e1 = A.do(act, E[:, 128:384], E[:, 128:384], ACT.Exp, bias=sc[:, 3:4],
                                  accum_out=sc[:, 5:6], w=[nm])
                        rr_ = V.do(rcp, sc[:, 6:8], sc[:, 4:6], w=[e0, e1])
                    else:
                        rr_ = soft(qa, ka, bias, Eb[i], sc, [qtok, ktok], [ef_[i]])
                    n0 = V.do(ts, Eb[i][:, 0:128], Eb[i][:, 0:128], sc[:, 6:7], None, ALU.mult, w=[rr_])
                    n1 = V.do(ts, Eb[i][:, 128:384], Eb[i][:, 128:384], sc[:, 7:8], None, ALU.mult, w=[rr_])
                    tE, tET = turn(Eb[i], ETb[j], [n0, n1], [etf_[j]])
                    ef_[i] = tE
                    et = [tET]
                P.wait(et, vtok)
                o = banks[ob[0]][p0:p0 + 64, 0:256]
                t = pv(o, VV[:, 0, 64 * h:64 * h + 64], VV[:, 1, 64 * h:64 * h + 64], ETb[j])
                etf_[j] = t
                if h % 2 == 1:
                    o_evac(h, ob[0], t)
            e_, new_ = x_add()
            proj_n("w_out_2", layer, 8, 0, 1024, mH_, mL_, mtok, e_)
            xt[0], xt[1] = new_

        for layer in range(2):
            swiglu(1, layer)
            attention(layer)
            swiglu(2, layer)

        SP.dma(out, X[:, :, :], s_out, w=[xt[0], xt[1]])
        SP.wait((s_out, 16))

        block = ctx.enter_context(nc.Block())

        @block.sync
        def _(e):
            SP.replay(e)

        @block.gpsimd
        def _(e):
            G.replay(e)

        @block.scalar
        def _(e):
            A.replay(e)

        @block.vector
        def _(e):
            V.replay(e)

        @block.tensor
        def _(e):
            P.replay(e)


def kernel(**inputs):
    import concourse.bacc as bacc
    from concourse.bass_utils import run_bass_kernel_spmd as run

    a = {k: np.asarray(v) for k, v in inputs.items()}
    plan = stream_plan()
    ws = np.empty((len(plan), 128, PIECE), np.float32)
    for i, (name, layer, k0, nk, c0, w) in enumerate(plan):
        m = a[name][layer][128 * k0:128 * (k0 + nk), c0:c0 + w]
        ws[i] = m.reshape(nk, 128, w).transpose(1, 0, 2).reshape(128, PIECE)
    CA, ncol = col_at()
    cols = np.concatenate([a[n].reshape(w, 128) for n, w in COLS], 0).T
    SA, ns = small_at()
    small = np.zeros((128, ns), np.float32)

    def put(name, v, r0=0):
        o, w = SA[name]
        v = v.reshape(-1, w)
        small[r0:r0 + (128 if v.shape[0] == 1 else v.shape[0]), o:o + w] = v

    put("lam", np.concatenate([a["lam_q1"][0], a["lam_k1"][0], a["lam_q2"][0], a["lam_k2"][0]]))
    for n, src in (("gq", "g_q_b_2"), ("gk", "g_k_b_2"), ("gqd", "g_q_d_2"), ("gkd", "g_k_d_2")):
        g = a[src][0]
        put(n, g)
        put(n + "s", np.concatenate([g[32:], g[:32]]))
    put("gqc", a["g_q_c_2"][0])
    put("gkc", a["g_k_c_2"][0])
    put("w2a2", np.concatenate([a["rwkv_w2"][0], a["rwkv_a2"][0]], 0))
    put("g2", a["rwkv_g2"][0])
    put("wf", a["w_in_cd_2"][0][:, 3072:3080].reshape(8, 128, 8).transpose(1, 0, 2).reshape(128, 64))
    put("bf", a["b_f_2"][0].reshape(8, 1))
    arrays = {
        "ws": ws,
        "xin": np.ascontiguousarray(a["x"][0].reshape(2, 128, D).transpose(1, 0, 2)),
        "pin": np.ascontiguousarray(a["p"][0, 0].T.reshape(2, 128, S).transpose(1, 0, 2)),
        "cols": np.ascontiguousarray(cols),
        "const": constants(),
        "small": small,
        "row": np.ascontiguousarray(np.broadcast_to(a["final_norm_g"], (128, D))),
    }
    nc = bacc.Bacc("TRN2", target_bir_lowering=False, num_devices=1)
    aps = [nc.dram_tensor(n, v.shape, mybir.dt.from_np(v.dtype), kind="ExternalInput").ap()
           for n, v in arrays.items()]
    out = nc.dram_tensor("out", (128, 2, D), F, kind="ExternalOutput").ap()
    program(nc, *aps, out)
    r = run(nc, [arrays], core_ids=[0])
    o = r.results[0]["out"]
    return o.transpose(1, 0, 2).reshape(1, S, D)
```

```python
import math
from contextlib import ExitStack

import numpy as np

import concourse.bass as bass
from concourse import mybir

F = mybir.dt.float32
R = mybir.dt.float32r
ALU = mybir.AluOpType
ACT = mybir.ActivationFunctionType
AX = mybir.AxisListType

S = 256
D = 1024
EPS = 1e-6
BIG = -1.0e30
GAMMA = math.exp(-0.5)
LN_SHIFT = 30.0 * math.log(2.0)

NRAW = 3
NSPL = 3
DEPTH = 6
LEADS = (0.3, 1.5, 0.6)
FINE = 2
RWKV_ORDER = (1536, 512, 768, 0, 256, 1024, 1280)
PIECE = 2048


def stream_plan():
    plan = []

    def cols(name, layer, kt, c0, n, w):
        for c in range(c0, c0 + n, w):
            plan.append((name, layer, 0, kt, c, w))

    def deep(name, layer, kt, c0, w=1024):
        per = PIECE // w
        for k in range(0, kt, per):
            plan.append((name, layer, k, per, c0, w))

    for c in RWKV_ORDER:
        cols("w_in", 0, 8, c, 256, 256)
    cols("w_in", 0, 8, 1792, 1024, 256)
    deep("w_in", 0, 8, 2816, 512)
    cols("w_in", 0, 8, 3328, 2048, 256)
    cols("w_proj_b", 0, 4, 0, 1024, 512)
    cols("w_proj_a", 0, 4, 0, 1024, 512)
    deep("w_out", 0, 8, 0)
    cols("w_ff1", 0, 8, 0, 4096, 256)
    deep("w_ff2", 0, 32, 0)
    deep("w_ple", 0, 2, 0)
    deep("w_ple_gate", 0, 8, 0)

    def ffn(n, layer):
        for c in range(0, 2816, 256):
            cols(f"ffn{n}_w_gate_2", layer, 8, c, 256, 256)
            cols(f"ffn{n}_w_up_2", layer, 8, c, 256, 256)
        deep(f"ffn{n}_w_down_2", layer, 22, 0)

    for layer in range(2):
        ffn(1, layer)
        if layer == 0:
            cols("w_in_ab_2", 0, 8, 0, 512, 256)
            cols("w_in_ab_2", 0, 8, 1024, 512, 256)
            deep("w_in_ab_2", 0, 8, 512, 512)
            deep("w_in_ab_2", 0, 8, 1536, 512)
            deep("w_in_ab_2", 0, 8, 2048)
        else:
            deep("w_in_cd_2", 0, 8, 0, 512)
            deep("w_in_cd_2", 0, 8, 1024, 512)
            deep("w_in_cd_2", 0, 8, 512, 512)
            deep("w_in_cd_2", 0, 8, 1536, 512)
            deep("w_in_cd_2", 0, 8, 2048)
        deep("w_out_2", layer, 8, 0)
        ffn(2, layer)
    return plan


COLS = [("norm_mix_g", 8), ("rwkv_mu", 14), ("rwkv_w0", 4), ("rwkv_a0", 4), ("rwkv_k_k", 4), ("rwkv_k_a", 4),
        ("rwkv_r_k", 4), ("rwkv_lnx_w", 4), ("rwkv_lnx_b", 4), ("diff_subln_g", 1), ("norm_mlp_g", 8),
        ("norm_ple_g", 8), ("norm_ffn1_2", 16), ("norm_mix_2", 16), ("norm_ffn2_2", 16), ("final_norm_g", 8)]


def col_at():
    at, n = {}, 0
    for name, w in COLS:
        at[name] = n
        n += w
    return at, n


CONSTS = [("ident", 128), ("strict", 128), ("incl", 128), ("dgt", 128), ("dgn", 128), ("ofn", 128),
          ("bones", 128), ("ones128", 128), ("ntri", 128), ("nones", 128), ("caus", 384), ("dil", 384),
          ("ndist", 384), ("cos", 128), ("sin", 128), ("eps", 8)]


def const_at():
    at, n = {}, 0
    for name, w in CONSTS:
        at[name] = (n, w)
        n += w
    return at, n


def constants():
    at, n = const_at()
    c = np.zeros((128, n), np.float32)

    def put(name, a):
        o, w = at[name]
        c[:a.shape[0], o:o + w] = a.reshape(a.shape[0], w)

    p = np.arange(128)
    put("ident", np.eye(128))
    put("strict", (p[:, None] < p[None, :]).astype(np.float32))
    put("incl", (p[:, None] <= p[None, :]).astype(np.float32))
    same = (p[:, None] // 16) == (p[None, :] // 16)
    put("dgt", ((p[:, None] < p[None, :]) & same).astype(np.float32))
    put("dgn", ((p[:, None] > p[None, :]) & same).astype(np.float32))
    put("ofn", ((p[:, None] > p[None, :]) & ~same).astype(np.float32))
    put("bones", ((p[:, None] // 64) == (p[None, :] // 64)).astype(np.float32))
    put("ones128", np.ones((128, 128)))
    put("ntri", -(p[:, None] >= p[None, :]).astype(np.float32))
    put("nones", -np.ones((128, 128)))
    d0 = p[:, None] - p[None, :]
    d1 = 128 + p[:, None] - np.arange(256)[None, :]
    dist = np.concatenate([d0, d1], 1)
    ok = dist >= 0
    put("caus", np.where(ok, 0.0, BIG))
    cnt = ((dist <= 128).astype(int) + (dist % 4 == 0) + (dist % 16 == 0)) * ok
    put("dil", np.where(cnt > 0, np.log(np.maximum(cnt, 1)), BIG))
    put("ndist", np.where(ok, -dist, 0))
    inv = 1.0 / (10000.0 ** (np.arange(0, 64, 2, dtype=np.float32) / np.float32(64)))
    ang = (np.arange(256, dtype=np.float32)[:, None] * inv.astype(np.float32)[None, :]).astype(np.float64)
    cs, sn = np.cos(ang), np.sin(ang)
    put("cos", np.concatenate([cs, cs], 1).reshape(2, 128, 64).transpose(1, 0, 2))
    put("sin", np.concatenate([-sn, sn], 1).reshape(2, 128, 64).transpose(1, 0, 2))
    put("eps", np.tile(np.array([EPS, 64 * 1e-5, 1e-5, LN_SHIFT / 2, 1.0, 0, 0, 0]), (128, 1)))
    return c


ROWS = [("final_norm_g", 1024)]
SMALL = [("lam", 256), ("gq", 64), ("gqs", 64), ("gk", 64), ("gks", 64),
         ("gqd", 64), ("gqds", 64), ("gkd", 64), ("gkds", 64), ("gqc", 64), ("gkc", 64),
         ("w2a2", 512), ("g2", 512), ("wf", 64), ("bf", 1)]


def small_at():
    at, n = {}, 0
    for name, w in SMALL:
        at[name] = (n, w)
        n += w
    return at, n


ENDS = {}
STEP = [0, 0.0]


def about(f, a):
    if f is table:
        return 1.3
    n = int(np.prod(a[0].shape[1:]))
    if f is mm:
        return n * (1 if a[1].dtype == R else 4) / 2400
    if f is tr:
        return n / 2400
    if f in (act, acopy):
        return 0.25 + n / 1200
    return 0.2 + n / 960


class Engine:

    def __init__(self, sem, linked=False):
        self.sem = sem
        self.linked = linked
        self.n = 0
        self.q = []
        self.passed = {}
        self.t = 0.0
        self.ready = 0.0

    def wait(self, *tokens):
        for t in tokens:
            if t is None:
                continue
            if isinstance(t, list):
                self.wait(*t)
                continue
            sem, value = t
            self.ready = max(self.ready, ENDS.get((id(sem), value), 0.0) + 0.1)
            if self.passed.get(id(sem), 0) < value:
                self.passed[id(sem)] = value
                self.q.append((_wait, (sem, value), {}, None))

    def do(self, f, *a, w=(), inc=True, **k):
        self.wait(*w)
        if self.linked and self.n:
            self.wait((self.sem, self.n))
        self.q.append((f, a, k, (self.sem, 1) if inc else None))
        self.t = max(self.t, self.ready) + about(f, a)
        self.ready = 0.0
        STEP[0] += 1
        STEP[1] = max(STEP[1], self.t)
        if inc:
            self.n += 1
            ENDS[id(self.sem), self.n] = self.t
            return (self.sem, self.n)
        return None

    def dma(self, out, in_, sem, w=()):
        self.wait(*w)
        self.q.append((_dma, (out, in_), {}, (sem, 16)))

    def replay(self, e):
        for f, a, k, inc in self.q:
            ins = f(e, *a, **k)
            if inc:
                ins.then_inc(inc[0], inc[1])


def _wait(e, sem, value):
    e.wait_ge(sem, value)


def _dma(e, out, in_):
    return e.dma_start(out, in_)


def bc(ap, dim, n):
    shape = list(ap.shape)
    shape[dim] = n
    return ap.broadcast_to(shape)


def table(e, name):
    e.preload_act_table_set(name)


def act(e, out, in_, func, **k):
    return e.activation(out, in_, func, **k)


def mm(e, out, a, b, start, stop):
    return e.matmul(out, a, b, start=start, stop=stop)


def tr(e, out, a, ident):
    return e.transpose(out, a, ident)


def cp(e, out, a):
    return e.tensor_copy(out, a)


def acopy(e, out, a):
    return e.copy(out, a)


def ts(e, out, a, s1, s2, op0, op1=None):
    if op1 is None:
        return e.tensor_scalar(out, a, s1, None, op0)
    return e.tensor_scalar(out, a, s1, s2, op0, op1)


def tt(e, out, a, b, op):
    return e.tensor_tensor(out, a, b, op)


def stt(e, out, a, s, b, op0, op1):
    return e.scalar_tensor_tensor(out=out, in0=a, scalar=s, in1=b, op0=op0, op1=op1)


def ttr(e, out, a, b, op0, op1, init, acc):
    return e.tensor_tensor_reduce(out, a, b, 1.0, init, op0, op1, acc)


def red(e, out, a, op):
    return e.tensor_reduce(out, a, AX.X, op)


def rcp(e, out, a):
    return e.reciprocal(out, a)


def scan(e, out, d0, d1, init, op0, op1):
    return e.tensor_tensor_scan(out, d0, d1, init, op0, op1)


def mset(e, out, v):
    return e.memset(out, v)


def program(nc, ws, xin, pin, colsin, constin, smallin, rowin, out):
    plan = stream_plan()
    CA, NCOL = col_at()
    KA, NK = const_at()
    SA, NS_ = small_at()
    with ExitStack() as ctx:
        def sem(name):
            return ctx.enter_context(nc.semaphore(name))

        P = Engine(sem("s_pe"))
        V = Engine(sem("s_dve"), linked=True)
        A = Engine(sem("s_act"), linked=True)
        G = Engine(sem("s_pool"))
        SP = Engine(sem("s_sp"))
        s_raw = [sem(f"s_raw{i}") for i in range(NRAW)]
        s_first = sem("s_first")
        s_x = [sem(f"s_x{b}") for b in range(2)]
        s_const = sem("s_const")
        s_row = sem("s_row")
        s_out = sem("s_out")

        base = (nc.sbuf_base + 63) // 64 * 64
        top = [base]

        def at(name, shape, dt, offset):
            return nc.alloc_sbuf_tensor_at(name, shape, dt, offset=offset)

        def fixed(name, shape, dt=F):
            size = 4 * int(np.prod(shape[1:]))
            t = at(name, shape, dt, top[0])
            top[0] += (size + 31) // 32 * 32
            return t

        raw = [fixed(f"raw{i}", [128, PIECE]) for i in range(NRAW)]
        hi = [fixed(f"hi{i}", [128, PIECE], R) for i in range(NSPL)]
        lo = [fixed(f"lo{i}", [128, PIECE], R) for i in range(NSPL)]
        X = fixed("X", [128, 2, D])
        HH = fixed("HH", [128, 8, S], R)
        HL = fixed("HL", [128, 8, S], R)
        cols = fixed("cols", [128, NCOL])
        const = fixed("const", [128, NK])
        small = fixed("small", [128, NS_])
        st = fixed("st", [128, 352])
        RB = fixed("RB", [128, S])
        nt = fixed("nt", [128, 512])
        arena0 = top[0]
        arena_end = nc.sbuf_usable_end
        names = [0]

        class Arena:
            def __init__(self, start=0):
                self.p = arena0 + start

            def __call__(self, shape, dt=F):
                size = 4 * int(np.prod(shape[1:]))
                names[0] += 1
                t = at(f"a{names[0]}", shape, dt, self.p)
                self.p += (size + 31) // 32 * 32
                assert self.p <= arena_end, (self.p - arena0, arena_end - arena0)
                return t

            def here(self):
                return self.p - arena0

        banks = [ctx.enter_context(nc.psum_tensor(f"ps{i}", [128, 512], F)) for i in range(8)]
        free = [(i, []) for i in range(8)]

        def take():
            return free.pop(0)

        def give(i, tokens):
            free.append((i, list(tokens)))

        def K(name, rows=128):
            o, w = KA[name]
            return const[0:rows, o:o + w]

        def SM(name, r0=0, r1=128):
            o, w = SA[name]
            return small[r0:r1, o:o + w]

        def col(name, i=0):
            o = CA[name] + i
            return cols[:, o:o + 1]

        ident = K("ident")

        def cK(name, i):
            o, _ = KA[name]
            return const[:, o + i:o + i + 1]

        eps6, epsgn, epssub, lnsh, one1 = [cK("eps", i) for i in range(5)]

        SP.dma(cols[:, :], colsin, s_first)
        SP.dma(ident, constin[:, 0:128], s_first)
        for b in range(2):
            SP.dma(X[:, b, :], xin[:, b, :], s_x[b])
        t_first = (s_first, 32)
        t_const = (s_const, 32)

        raw_tok = {}
        spl_tok = {}
        raw_free = [[] for _ in range(NRAW)]
        issued = [0]
        cursor = [0]
        splits = [0]
        half_split = []

        def issue():
            i = issued[0]
            if i >= len(plan):
                return
            s = i % NRAW
            SP.dma(raw[s][:, :], ws[i], s_raw[s], w=raw_free[s])
            raw_tok[i] = (s_raw[s], 16 * (i // NRAW + 1))
            issued[0] += 1

        def split_hi(after):
            i = splits[0]
            if i >= len(plan):
                return
            s = i % NSPL
            ta = A.do(acopy, hi[s][:, :], raw[i % NRAW][:, :], w=[raw_tok[i], after])
            splits[0] += 1
            half_split.append((i, ta, after))

        def split_lo():
            if not half_split:
                return
            i, ta, after = half_split.pop(0)
            s = i % NSPL
            r = raw[i % NRAW]
            tv = V.do(tt, lo[s][:, :], r[:, :], hi[s][:, :].bitcast(F), ALU.subtract, w=[raw_tok[i], after, ta])
            spl_tok[i] = [ta, tv]
            raw_free[i % NRAW] = [ta, tv]
            issue()

        issue()
        issue()
        SP.dma(const[:, 128:NK], constin[:, 128:NK], s_const)
        SP.dma(small[:, :], smallin, s_const)
        for _ in range(NRAW - 2):
            issue()

        def piece(name, layer, kt, c):
            i = cursor[0]
            while i not in spl_tok:
                split_lo()
            n, ly, k0, nk, c0, w = plan[i]
            assert (n, ly, k0, c0) == (name, layer, kt, c), (plan[i], name, layer, kt, c)
            P.wait(spl_tok[i])
            s = i % NSPL
            return (hi[s][:, :].rearrange("p (k n) -> p k n", k=nk),
                    lo[s][:, :].rearrange("p (k n) -> p k n", k=nk))

        def done(tok):
            cursor[0] += 1
            release(tok)

        def release(tok):
            split_lo()
            split_hi(tok)

        def mm3(o, ah, al, bh, bl, start, stop, inc=False):
            P.do(mm, o, ah, bh, start, False, inc=False)
            P.do(mm, o, ah, bl, False, False, inc=False)
            return P.do(mm, o, al, bh, False, stop, inc=stop or inc)

        def last_pe():
            return (P.sem, P.n)

        def run(*tracks, fill=(), pool=(), depth=0, lead=0.0):
            pool = list(pool)
            live = [[t, False, 0.0, False] for t in tracks] + [[t, True, 0.0, False] for t in fill]
            pooled = []
            idle = 0
            while live or pool:
                while pool and len(pooled) < depth:
                    e = [pool.pop(0), False, P.t, False]
                    live.append(e)
                    pooled.append(e)
                ready = [e for e in live if not e[3]]
                if not ready:
                    idle += 1
                    assert idle < 40
                    for e in live:
                        e[3] = False
                    continue
                e = min(ready, key=lambda e: P.t + lead if e[1] else e[2])
                n, STEP[1] = STEP[0], 0.0
                try:
                    next(e[0])
                except StopIteration:
                    live.remove(e)
                    if e in pooled:
                        pooled.remove(e)
                    n = -1
                if STEP[0] == n:
                    e[3] = True
                else:
                    idle = 0
                    e[2] = STEP[1] if STEP[0] != n else e[2]
                    for x in live:
                        x[3] = False

        def proj_t(name, layer, c, sh, sl, w, nk, deps, evac):
            wh, wl = piece(name, layer, 0, c)
            for j in range(0, w, 256):
                b, fr = take()
                P.wait(fr)
                o = banks[b][:, :].rearrange("p (a n) -> p a n", a=2)
                for u in range(2):
                    for k in range(nk):
                        a, z = j + 128 * u, j + 128 * u + 128
                        P.wait(need(deps[k]))
                        t = mm3(o[:, u, :], wh[:, k, a:z], wl[:, k, a:z], sh[:, k, :], sl[:, k, :],
                                k == 0, k == nk - 1)
                        if k % FINE == FINE - 1 and (u, k) != (1, nk - 1):
                            yield
                if j + 256 >= w:
                    done(t)
                held_evacs.append((b, evac, o, c + j, t))
                if not late or len(held_evacs) > 1:
                    run_late()
                    while held_evacs:
                        b, e_, o, n, t = held_evacs.pop(0)
                        give(b, e_(o, n, t))
                if j + 256 >= w:
                    split_lo()
                yield

        def need(d, b=None):
            if isinstance(d, dict):
                return d[b] if b is not None else list(d.values())
            return d

        late = []
        held_evacs = []

        def room(n):
            while len(free) < n:
                yield

        cur_bank = [None]

        def run_late():
            while late:
                late.pop(0)()

        def proj_n(name, layer, kts, c, width, sh, sl, deps, evac, group=0, nm=None, between=iter(())):
            per = PIECE // width
            nh = width // 512
            bk = [take() for _ in range(2 * nh)]
            np_ = kts // per
            group = max(group, 1)

            def part(n, wh, wl, b, h, inc):
                k0 = n * per
                o = banks[bk[nh * b + h][0]][:, :]
                for k in range(per):
                    while isinstance(deps, dict) and k0 + k not in deps:
                        yield
                    P.wait(need(deps[k0 + k], b))
                    tok = slice(128 * b, 128 * b + 128)
                    t = mm3(o, sh[:, k0 + k, tok], sl[:, k0 + k, tok],
                            wh[:, k, 512 * h:512 * h + 512], wl[:, k, 512 * h:512 * h + 512],
                            k0 + k == 0, k0 + k == kts - 1, inc and k == per - 1)
                    yield
                return t

            for n in range(np_ - group):
                wh, wl = piece(name, layer, per * n, c)
                if n == 0:
                    for _, fr in bk:
                        P.wait(fr)
                for b in range(2):
                    for h in range(nh):
                        t = yield from part(n, wh, wl, b, h, b == 1 and h == nh - 1)
                done(t)
                split_lo()
            ps = []
            for n in range(np_ - group, np_):
                ps.append(piece(name, layer, per * n, c))
                cursor[0] += 1
            cursor[0] -= group
            if np_ == group:
                for _, fr in bk:
                    P.wait(fr)
            owed = []
            for b in range(2):
                for h in range(nh):
                    last = b == 1 and h == nh - 1
                    for q, (wh, wl) in enumerate(ps):
                        t = yield from part(np_ - group + q, wh, wl, b, h, last)
                        if last:
                            owed.append(t)
                        if nm and (b, h) == (1, 0) and q == 0:
                            nm.part(0, 0)
                    if last and not nm:
                        for x in owed:
                            done(x)
                    run_late()
                    cur_bank[0] = bk[nh * b + h][0]
                    reads = evac(banks[cur_bank[0]][:, :], b, h, t)
                    if reads is not None:
                        give(bk[nh * b + h][0], reads)
                    if nm and last:
                        cursor[0] += group
                        nm.part(1, 0)
                        for _ in range(2):
                            next(between, None)
                        nm.stat(b, h)
                        nm.part(1, 1)
                        release(owed.pop(0))
                        nm.end()
                        for x in owed:
                            release(x)
                        rows = late[:]
                        late.clear()
                        for _ in between:
                            pass
                        late.extend(rows)
                    elif nm:
                        nm.stat(b, h)
                        if (b, h) == (1, 0):
                            nm.part(0, 1)
                    split_lo()
                    yield

        xt = {(b, h): [(s_x[b], 16)] for b in range(2) for h in range(2)}
        h_free = [None]
        rb_free = [[]]
        rstd = [st[:, 4:5], st[:, 5:6]]

        def newton(y, m, t, u, w):
            k = V.do(tt, t, y, y, ALU.mult, w=w)
            k = V.do(tt, t, t, m, ALU.mult, w=[k])
            k = V.do(ts, t, t, -0.5, 1.5, ALU.mult, ALU.add, w=[k])
            return V.do(tt, u, y, t, ALU.mult, w=[k])

        nt_free = [None]

        class Norm:

            early_table = True

            def __init__(self, gname, gi=0):
                self.g = cols[:, CA[gname] + gi:CA[gname] + gi + 8]
                self.h = {k: {} for k in range(8)}
                self.r = []
                self.s = []
                self.bank = None

            def part(self, b, h):
                bb, fr = take()
                P.wait(fr, xt[b, h], t_first)
                for u in range(4):
                    c = 512 * h + 128 * u
                    t = P.do(tr, banks[bb][:, 128 * u:128 * u + 128], X[:, b, c:c + 128], ident, inc=(u == 3))
                n4 = nt[:, :].rearrange("p (u n) -> p u n", u=4)
                g = self.g[:, 4 * h:4 * h + 4].rearrange("p (k o) -> p k o", o=1)
                hh = HH[:, 4 * h:4 * h + 4, 128 * b:128 * b + 128]
                hl = HL[:, 4 * h:4 * h + 4, 128 * b:128 * b + 128]
                t1 = V.do(tt, n4, banks[bb][:, :].rearrange("p (u n) -> p u n", u=4), bc(g, 2, 128), ALU.mult,
                          w=[t, nt_free[0]])
                give(bb, [t1])
                self.turned = t
                t2 = A.do(acopy, hh, n4, w=[t1, h_free[0]])
                t3 = V.do(tt, hl, n4, hh.bitcast(F), ALU.subtract, w=[t2, h_free[0]])
                for k in range(4 * h, 4 * h + 4):
                    self.h[k][b] = [t2, t3]

            def stat(self, b, h):
                if not self.s:
                    self.bank, fr = take()
                    self.s = [fr]
                    if self.early_table:
                        A.do(table, "natural_log_exp_and_others", inc=False)
                i = 2 * b + h
                self.s.append(A.do(act, banks[self.bank][:, :], X[:, b, 512 * h:512 * h + 512], ACT.Square,
                                   accum_out=st[:, i:i + 1], w=[xt[b, h], self.s[0]]))

            def end(self):
                give(self.bank, [self.s[-1]])
                s2 = st[:, 0:4].rearrange("p (b h) -> p b h", b=2)
                t = V.do(red, st[:, 10:12], s2, ALU.add, w=[self.s[1:]])
                t = V.do(ts, st[:, 2:4], st[:, 10:12], 1.0 / D, EPS, ALU.mult, ALU.add, w=[t])
                t1 = A.do(act, st[:, 6:8], st[:, 2:4], ACT.Ln, w=[t])
                t1 = A.do(act, st[:, 6:8], st[:, 6:8], ACT.Exp, scale=-0.5, w=[t1])
                self.r.append(newton(st[:, 6:8], st[:, 2:4], st[:, 8:10], st[:, 4:6], [t1, rb_free[0]]))
                late.append(self.rows)

            def rows(self):
                b, fr = take()
                dg = nt[:, 0:256].rearrange("p (b n) -> p b n", b=2)
                for q in range(2):
                    td = V.do(ts, dg[:, q, :], ident, rstd[q], None, ALU.mult, w=[self.r[0], self.h[7][1]])
                P.wait(fr, td, t_const)
                for q in range(2):
                    t = P.do(mm, banks[b][:, 128 * q:128 * q + 128], K("ones128"), dg[:, q, :], True, True)
                nt_free[0] = t
                t = V.do(cp, RB[:, :], banks[b][:, 0:256], w=[t, rb_free[0]])
                give(b, [t])
                self.r.append(t)

        class FinalNorm(Norm):

            early_table = False

            def __init__(self, gname, frow, fdep):
                Norm.__init__(self, gname)
                f = CA["final_norm_g"]
                self.t = V.do(tt, st[:, 150:158], self.g, cols[:, f:f + 8], ALU.mult, w=[t_first])
                self.g = st[:, 150:158]
                self.frow, self.fdep = frow, fdep
                self.s2 = []
                self.left = []

            def part(self, b, h):
                Norm.part(self, b, h)
                if b == 0:
                    self.gain(b, h, self.turned)
                else:
                    self.left.append((b, h, self.turned))

            def gain(self, b, h, turned):
                o = slice(512 * h, 512 * h + 512)
                t = V.do(tt, X[:, b, o], X[:, b, o], self.frow[:, o], ALU.mult,
                         w=[turned, self.s[1 + 2 * b + h], self.fdep])
                i = 160 + 2 * b + h
                self.s2.append(A.do(act, banks[self.bank][:, :], X[:, b, o], ACT.Square,
                                    accum_out=st[:, i:i + 1], w=[t]))

            def end(self):
                A.do(table, "natural_log_exp_and_others", inc=False)
                for x in self.left:
                    self.gain(*x)
                give(self.bank, [self.s2[-1]])
                y1, y2, m, n, u = (st[:, i:i + 2] for i in (164, 166, 168, 170, 172))

                def mean(o, i, w):
                    s_ = st[:, i:i + 4].rearrange("p (b h) -> p b h", b=2)
                    t = V.do(red, o, s_, ALU.add, w=[w])
                    return V.do(ts, o, o, 1.0 / D, EPS if i == 0 else 0.0, ALU.mult, ALU.add, w=[t])

                def rs(y, x, t, to_, w):
                    t = A.do(act, y, x, ACT.Ln, w=[t])
                    t = A.do(act, y, y, ACT.Exp, scale=-0.5, w=[t])
                    return newton(y, x, u, to_, [t, w])

                t = mean(m, 0, self.s[1:])
                t1 = rs(st[:, 6:8], m, t, y1, None)
                t2 = mean(n, 160, self.s2)
                t = V.do(tt, n, n, y1, ALU.mult, w=[t1, t2])
                t = V.do(tt, n, n, y1, ALU.mult, w=[t])
                t = V.do(ts, n, n, EPS, None, ALU.add, w=[t])
                t = rs(st[:, 6:8], n, t, y2, None)
                self.r.append(V.do(tt, st[:, 4:6], y1, y2, ALU.mult, w=[t, rb_free[0]]))
                late.append(self.rows)
                for b in range(2):
                    t = A.do(act, X[:, b, :], X[:, b, :], ACT.Copy, scale=y1[:, b:b + 1], w=[t1, self.s2])
                    xt[b, 0] = xt[b, 1] = [t]

        RB2 = bc(RB[:, :].rearrange("p (o n) -> p o n", o=1), 1, 2)

        def x_add(factor=1.0):

            def evac(o, b, h, t):
                xb = X[:, b, 512 * h:512 * h + 512]
                tv = V.do(stt, xb, o, factor, xb, ALU.mult, ALU.add, w=[t, xt[b, h]])
                xt[b, h] = [tv]
                return [tv]
            return evac

        def halve(h, l, src, w):
            th = A.do(acopy, h, src, w=w)
            split_lo()
            return [th, V.do(tt, l, src, h.bitcast(F), ALU.subtract, w=[th, *w])]

        nm = Norm("norm_mix_g")
        nm.part(0, 0)
        nm.part(0, 1)
        split_hi(None)
        nm.part(1, 0)
        nm.part(1, 1)
        split_lo()
        nm.stat(0, 0)
        nm.stat(0, 1)
        split_hi(None)
        nm.stat(1, 0)
        nm.stat(1, 1)
        split_lo()
        nm.end()
        split_hi(None)
        split_lo()
        hdep, rdep = nm.h, nm.r

        ar = Arena()
        C = ar([128, 14, S])
        ub = [ar([128, 2, S + 1]) for _ in range(2)]
        dtmp = ar([128, 2, S])
        low = ar.here()
        tz = [V.do(mset, ub[i][:, :, 0:1], 0.0) for i in range(2)]
        o_ = CA["rwkv_mu"]
        t_om = V.do(ts, st[:, 128:142], cols[:, o_:o_ + 14], -1.0, 1.0, ALU.mult, ALU.add, w=[t_first])
        c_tok = {}
        u_free = [None, None]

        def shift_evac(o, c, t):
            i = (c // 256) % 2
            ta = V.do(tt, ub[i][:, :, 1:S + 1], o, RB2, ALU.mult, w=[t, tz[i], u_free[i], rdep])
            th = [A.do(act, C[:, c // 128 + u, :], ub[i][:, u, 1:S + 1], ACT.Copy,
                       scale=st[:, 128 + c // 128 + u:129 + c // 128 + u], w=[ta, t_om]) for u in range(2)]
            split_lo()
            for u in range(2):
                n = c // 128 + u
                tv = V.do(stt, C[:, n, :], ub[i][:, u, 0:S], col("rwkv_mu", n), C[:, n, :],
                          ALU.mult, ALU.add, w=[th[u]])
                c_tok[n] = tv
            u_free[i] = tv
            return [ta]


        rT, kT, vT = C[:, 0:4, :], C[:, 4:8, :], C[:, 8:12, :]
        AR = ar([128, 4, 2, 2, 128])
        BT = ar([128, 4, 2, 128])
        KT = ar([128, 4, 2, 128])
        BON = ar([128, 4, S])
        VN = ar([128, 2, 512])
        keep = ar.here()
        sw = ar([128, 4, S])
        cum = ar([128, 4, 2, 128])
        EP = ar([128, 4, 2, 128])
        aa = ar([128, 4, S])
        kkb = ar([128, 4, S])
        sq = ar([128, 4, S])
        vend = ar.here()
        YT = BT[:, :, :, :].rearrange("p c b n -> p c (b n)")
        uar = Arena(keep)
        BKN = uar([128, 2, 512])
        US = uar([128, 2, 4, 64])
        SS = uar([128, 4, 64])
        c_ar = Arena(0)
        d_ar = Arena(14 * 4 * S)
        T = [c_ar([128, 4, 128]) for _ in range(6)] + [d_ar([128, 4, 128])]
        PER = [d_ar([128, 4, 128]) for _ in range(2)] + [uar([128, 4, 128]) for _ in range(3)]
        uend = uar.here()
        assert c_ar.here() <= 13 * 4 * S and d_ar.here() <= low
        oaH = Arena(0)([128, 4, S], R)
        oaL = Arena(4 * 1024)([128, 4, S], R)
        dar = Arena(vend)
        qT = dar([128, 4, S])
        kTt = dar([128, 4, S])
        vN = dar([128, 2, 512])
        obH = dar([128, 4, S], R)
        obL = dar([128, 4, S], R)
        ear = Arena(uend)
        Es = [ear([128, 384]) for _ in range(2)]
        ETs = ear([128, 384])
        AB = ear([128, 384])
        oT = ear([128, S])
        sqd = ear([128, S])
        assert ear.here() <= vend
        gB = Arena(vend)([128, 8, S])
        gA = X[:, :, :].rearrange("p b (n s) -> p (b n) s", s=S)
        sg = C[:, 13, :]
        R_ = {}

        def b4(i):
            return banks[i][:, :].rearrange("p (u n) -> p u n", u=4)

        def bm(name):
            return bc(K(name).rearrange("p (o n) -> p o n", o=1), 1, 4)

        def have(a, b):
            while any(n not in c_tok for n in range(a, b)):
                yield
            return [c_tok[n] for n in range(a, b)]

        def rwkv():
            ct = yield from have(12, 14)
            t12 = A.do(act, C[0:64, 12, :], C[0:64, 12, :], ACT.Tanh, w=ct)
            tsg = A.do(act, sg, sg, ACT.Sigmoid, w=ct)
            R_["tsg"] = tsg
            a_tok, w_tok = [], []
            yield
            for c2 in range(2):
                bw, fw = take()
                ba, fa = take()
                P.wait(fw, fa, t12, ct, t_const)
                for u in range(2):
                    c = 2 * c2 + u
                    o = slice(256 * u, 256 * u + 256)
                    w_ = SM("w2a2")[:, 128 * c:128 * c + 128]
                    P.do(mm, banks[bw][:, o], w_[0:64, :], C[0:64, 12, :], True, True, inc=False)
                    t = P.do(mm, banks[ba][:, o], w_[64:128, :], C[64:128, 12, :], True, True)
                for u in range(2):
                    c = 2 * c2 + u
                    o = slice(256 * u, 256 * u + 256)
                    w_tok.append(A.do(act, sw[:, c, :], banks[bw][:, o], ACT.Sigmoid, bias=col("rwkv_w0", c),
                                      w=[t, R_["free"]]))
                    a_tok.append(A.do(act, aa[:, c, :], banks[ba][:, o], ACT.Sigmoid, bias=col("rwkv_a0", c),
                                      w=[t, R_["free"]]))
                give(bw, w_tok[-2:])
                give(ba, a_tok[-2:])
                yield
            A.do(table, "natural_log_exp_and_others", inc=False)
            sw4 = sw[:, :, :].rearrange("p c (b n) -> p c b n", b=2)
            ones = K("ones128")
            tcs = []
            for c in range(4):
                for b in range(2):
                    tcs.append(V.do(scan, cum[:, c, b, :], ones, sw4[:, c, b, :], 0.0, ALU.mult, ALU.add,
                                    w=[w_tok[c], t_const]))
            mid = st[:, 16:24].rearrange("p (c b o) -> p c b o", c=4, b=2)
            tm = V.do(cp, mid, cum[:, :, :, 63:64], w=[tcs])
            tem = A.do(act, st[:, 24:32], st[:, 16:24], ACT.Exp, scale=-GAMMA, w=[tm])
            yield
            tcc = V.do(tt, cum[:, :, :, :], cum[:, :, :, :], bc(mid, 3, 128), ALU.subtract, w=[tm, tcs])
            tep = A.do(act, EP[:, :, :, :], cum[:, :, :, :], ACT.Exp, scale=-GAMMA, w=[tcc])
            tcx = V.do(tt, sw4, cum[:, :, :, :], sw4, ALU.subtract, w=[tcc, tcs])
            yield
            ctk = yield from have(4, 8)
            tk, tsq = [], []
            ka0, kk0 = CA["rwkv_k_a"], CA["rwkv_k_k"]
            tng = V.do(ts, st[:, 142:146], cols[:, kk0:kk0 + 4], -1.0, None, ALU.mult, w=[t_first])
            tng = V.do(ts, st[:, 146:150], cols[:, ka0:ka0 + 4], -1.0, 1.0, ALU.mult, ALU.add, w=[tng])
            for c in range(4):
                t1 = A.do(act, kkb[:, c, :], kT[:, c, :], ACT.Copy, scale=st[:, 142 + c:143 + c],
                          w=[ctk, tng, R_["free"]])
                tsq.append(A.do(act, sq[:, c, :], kkb[:, c, :], ACT.Square, w=[t1, R_["free"]]))
            yield
            for c in range(4):
                b, fr = take()
                t3 = P.do(mm, banks[b][:, 0:256], K("bones"), sq[:, c, :], True, True, w=[fr, tsq[c]])
                t4 = V.do(ts, sq[:, c, :], banks[b][:, 0:256], 1e-24, None, ALU.max, w=[t3])
                give(b, [t4])
                tk.append(t4)
                if c == 1:
                    yield
            tl = A.do(act, sq[:, :, :], sq[:, :, :], ACT.Ln, scale=float(2 ** 30), w=[tk])
            tl = A.do(act, sq[:, :, :], sq[:, :, :], ACT.Exp, scale=-0.5, bias=lnsh, w=[tl])
            yield
            r4 = rT.rearrange("p c (b n) -> p c b n", b=2)
            k4 = kT.rearrange("p c (b n) -> p c b n", b=2)
            tkk = V.do(tt, kkb[:, :, :], kkb[:, :, :], sq[:, :, :], ALU.mult, w=[tl])
            yield
            ctr = yield from have(0, 4)
            trho = V.do(tt, AR[:, :, :, 1, :], r4, EP[:, :, :, :], ALU.mult, w=[tep, ctr])
            tend = V.do(cp, st[:, 32:36].rearrange("p (c o) -> p c o", o=1), EP[:, :, 0, 127:128], w=[tep])
            yield
            txp = A.do(act, EP[:, :, :, :], sw4, ACT.Exp, scale=-GAMMA, w=[tcx, trho, tend])
            tin = A.do(act, cum[:, :, :, :], cum[:, :, :, :], ACT.Exp, scale=GAMMA, w=[tep, tcx])
            for c in range(4):
                t1 = A.do(act, sq[:, c, :], aa[:, c, :], ACT.Identity, scale=col("rwkv_k_a", c),
                          bias=st[:, 146 + c:147 + c], w=[tkk, a_tok])
            tk2 = V.do(tt, kT, sq[:, :, :], kT, ALU.mult, w=[t1])
            yield
            kk4 = kkb[:, :, :].rearrange("p c (b n) -> p c b n", b=2)
            talpha = V.do(tt, AR[:, :, :, 0, :], kk4, EP[:, :, :, :], ALU.mult, w=[txp, tkk])
            yield
            tb = V.do(stt, kkb[:, :, :], kkb[:, :, :], -1.0, aa[:, :, :], ALU.mult, ALU.mult, w=[talpha, a_tok])
            tbeta = V.do(tt, BT[:, :, :, :], kk4, cum[:, :, :, :], ALU.mult, w=[tb, tin])
            yield
            tkap = V.do(tt, KT[:, :, :, :], k4, cum[:, :, :, :], ALU.mult, w=[tk2, tin])
            yield
            trk = []
            for c in range(4):
                trk.append(V.do(stt, sq[:, c, :], rT[:, c, :], col("rwkv_r_k", c), kT[:, c, :], ALU.mult,
                                ALU.mult, w=[tk2]))
            ctv = yield from have(8, 12)
            tvn = []
            for q in range(2):
                b, fr = take()
                P.wait(fr, ctv)
                for c in range(4):
                    t = P.do(tr, banks[b][:, 128 * c:128 * c + 128], vT[:, c, 128 * q:128 * q + 128], ident,
                             inc=(c == 3))
                tvn.append(A.do(acopy, VN[:, q, :], banks[b][:, :], w=[t]))
                give(b, [tvn[-1]])
            yield
            for c in range(4):
                b, fr = take()
                t2 = P.do(mm, banks[b][:, 0:256], K("bones"), sq[:, c, :], True, True, w=[fr, trk[c]])
                tbon = V.do(tt, BON[:, c, :], banks[b][:, 0:256], vT[:, c, :], ALU.mult, w=[t2])
                give(b, [tbon])
                if c % 2:
                    yield
            u_start = [tbon, tkap, tbeta, talpha, trho, tin, tvn]
            R_["u_start"] = u_start
            R_["tbon"] = tbon
            tbk = []
            for n, src in enumerate((BT, KT)):
                b, fr = take()
                P.wait(fr, tbeta, tkap)
                for c in range(4):
                    t = P.do(tr, banks[b][:, 128 * c:128 * c + 128], src[:, c, 0, :], ident, inc=(c == 3))
                tbk.append(A.do(acopy, BKN[:, n, :], banks[b][:, :], w=[t, u_start]))
                give(b, [tbk[-1]])
            yield
            RBT, AKT, RKT, X8, Y1 = PER
            T0, T1, T2, T3, T4, T5, T6 = T
            ty = []
            free_ = u_start
            for g in range(2):
                t_state = None
                for blk in range(2):
                    sb = []
                    bs = [take() for _ in range(5)]
                    P.wait([f for _, f in bs], u_start)
                    bs = [b for b, _ in bs]
                    al, rh, be, ka = (lambda i: AR[64 * g:64 * g + 64, i, blk, 0, :],
                                      lambda i: AR[64 * g:64 * g + 64, i, blk, 1, :],
                                      lambda i: BT[64 * g:64 * g + 64, i, blk, :],
                                      lambda i: KT[64 * g:64 * g + 64, i, blk, :])
                    for bb, (l, r) in zip(bs, ((be, al), (al, be), (be, rh), (ka, al), (ka, rh))):
                        for i in range(4):
                            t = P.do(mm, banks[bb][:, 128 * i:128 * i + 128], l(i), r(i), True, True, inc=(i == 3))
                        sb.append(t)
                    dT = V.do(tt, T0[:, :, :], b4(bs[0]), bm("dgt"), ALU.mult, w=[sb[0], free_])
                    x1 = V.do(tt, T5[:, :, :], T0[:, :, :], bm("ident"), ALU.add, w=[dT, free_])
                    dN = V.do(tt, T1[:, :, :], b4(bs[1]), bm("dgn"), ALU.mult, w=[sb[1], free_])
                    give(bs[0], [dT])
                    lN = V.do(tt, T2[:, :, :], b4(bs[1]), bm("ofn"), ALU.mult, w=[sb[1], free_])
                    give(bs[1], [dN, lN])
                    rb = V.do(tt, RBT[:, :, :], b4(bs[2]), bm("incl"), ALU.mult, w=[sb[2], free_])
                    give(bs[2], [rb])
                    ak = V.do(tt, AKT[:, :, :], b4(bs[3]), bm("strict"), ALU.mult, w=[sb[3], free_])
                    give(bs[3], [ak])
                    rk = V.do(tt, RKT[:, :, :], b4(bs[4]), bm("incl"), ALU.mult, w=[sb[4], free_])
                    give(bs[4], [rk])
                    yield

                    def prod(l, r, deps):
                        b, fr = take()
                        P.wait(fr, *deps)
                        for i in range(4):
                            t = P.do(mm, banks[b][:, 128 * i:128 * i + 128], l[:, i, :], r[:, i, :], True, True,
                                     inc=(i == 3))
                        return b, t

                    def to(eng, dst, bt_, extra=None, more=()):
                        b, t = bt_
                        if extra is not None:
                            k = V.do(tt, dst[:, :, :], b4(b), extra, ALU.add, w=[t, *more])
                        elif eng is A:
                            k = A.do(acopy, dst[:, :, :], b4(b), w=[t, *more])
                        else:
                            k = V.do(cp, dst[:, :, :], b4(b), w=[t, *more])
                        give(b, [k])
                        return k

                    p1 = prod(T0, T1, [dT, dN])
                    d2 = to(A, T3, p1, more=[free_])
                    p2 = prod(T1, T0, [dT, dN])
                    d2t = to(A, T4, p2, more=[free_])
                    yield
                    p3 = prod(T3, T5, [d2, x1])
                    x2 = to(V, T0, p3, T5[:, :, :], [x1, p1[1], p2[1]])
                    p4 = prod(T4, T3, [d2t])
                    d4 = to(A, T1, p4, more=[p2[1]])
                    p5 = prod(T3, T4, [d2t])
                    d4t = to(A, T6, p5, more=[free_])
                    yield
                    p6 = prod(T1, T0, [d4, x2])
                    x4 = to(V, T5, p6, T0[:, :, :], [p3[1]])
                    p7 = prod(T6, T1, [d4t])
                    d8 = to(A, T3, p7, more=[p5[1]])
                    yield
                    p8 = prod(T3, T5, [d8, x4])
                    x8 = to(V, X8, p8, T5[:, :, :], [x4, free_])
                    yield
                    p9 = prod(X8, T2, [x8, lN])
                    n1 = to(A, T0, p9, more=[p6[1], x4])
                    p10 = prod(T2, X8, [x8, lN])
                    n1t = to(V, T1, p10, more=[p7[1]])
                    yield
                    p11 = prod(T1, T0, [n1, n1t])
                    n2 = to(A, T3, p11, more=[p8[1]])
                    p12 = prod(T0, T1, [n1, n1t])
                    n2t = to(V, T4, p12, more=[p5[1]])
                    yield
                    p13 = prod(T3, T4, [n2, n2t])
                    y4 = to(V, T5, p13, bm("ident"), [p8[1], x8])
                    yield
                    p14 = prod(T3, T5, [y4])
                    y2 = to(V, T6, p14, T5[:, :, :], [y4, p7[1]])
                    yield
                    p15 = prod(T0, T6, [y2])
                    y1 = to(V, Y1, p15, T6[:, :, :], [y2, free_])
                    yield
                    for k, (src, dep) in enumerate(((AKT, ak), (X8, x8), (Y1, y1))):
                        b, fr = take()
                        P.wait(fr, dep, tu if k else tvn)
                        for i in range(4):
                            h = 2 * i + g
                            o = banks[b][:, 64 * i:64 * i + 64]
                            if k == 0:
                                t = P.do(mm, o, src[:, i, :], VN[:, blk, 64 * h:64 * h + 64], True, blk == 0)
                                if blk == 1:
                                    P.wait(t_state)
                                    t = P.do(mm, o, AR[64 * g:64 * g + 64, i, 1, 0, :],
                                             SS[64 * g:64 * g + 64, i, :], False, True)
                            else:
                                t = P.do(mm, o, src[:, i, :], US[:, k % 2, i, :], True, True)
                        tu = A.do(acopy, US[:, (k + 1) % 2, :, :],
                                  banks[b][:, 0:256].rearrange("p (i d) -> p i d", i=4), w=[t, free_])
                        give(b, [tu])
                        yield
                    b, fr = take()
                    P.wait(fr, tu, rb, rk)
                    for i in range(4):
                        h = 2 * i + g
                        o = banks[b][64 * g:64 * g + 64, 128 * i:128 * i + 128]
                        P.do(mm, o, US[:, 1, i, :], RBT[:, i, :], True, False, inc=False)
                        t = P.do(mm, o, VN[:, blk, 64 * h:64 * h + 64], RKT[:, i, :], False, blk == 0)
                        if blk == 1:
                            t = P.do(mm, o, SS[64 * g:64 * g + 64, i, :], AR[64 * g:64 * g + 64, i, 1, 1, :],
                                     False, True)
                    y = A.do(acopy, YT[64 * g:64 * g + 64, :, 128 * blk:128 * blk + 128],
                             banks[b][64 * g:64 * g + 64, :].rearrange("p (u n) -> p u n", u=4), w=[t])
                    give(b, [y])
                    ty.append(y)
                    if blk == 0:
                        b, fr = take()
                        P.wait(fr, tbk)
                        for i in range(4):
                            h = 2 * i + g
                            o = banks[b][64 * g:64 * g + 64, 64 * i:64 * i + 64]
                            P.do(mm, o, BKN[:, 0, 64 * h:64 * h + 64], US[:, 1, i, :], True, False, inc=False)
                            t = P.do(mm, o, BKN[:, 1, 64 * h:64 * h + 64], VN[:, 0, 64 * h:64 * h + 64],
                                     False, True)
                        t_state = []
                        for i in range(4):
                            t_state.append(V.do(ts, SS[64 * g:64 * g + 64, i, :],
                                                banks[b][64 * g:64 * g + 64, 64 * i:64 * i + 64],
                                                st[64 * g:64 * g + 64, 32 + i:33 + i],
                                                st[64 * g:64 * g + 64, 25 + 2 * i:26 + 2 * i],
                                                ALU.mult, ALU.mult, w=[t, tem, tend]))
                        give(b, t_state)
                    free_ = [t]
                    yield
            far = Arena(keep)
            m1 = far([128, 4, S])
            m2 = far([128, 4, S])
            assert far.here() <= uend
            oa_tok = []
            sq_, gp = [], []
            for c in range(4):
                sq_.append(A.do(act, m2[:, c, :], YT[:, c, :], ACT.Square, w=[ty, t]))
            yield
            for c in range(4):
                b, fr = take()
                P.do(mm, banks[b][:, 0:256], K("bones"), YT[:, c, :], True, True, w=[fr, ty], inc=False)
                t1 = P.do(mm, banks[b][:, 256:512], K("bones"), m2[:, c, :], True, True, w=[sq_[c]])
                t2 = A.do(act, m1[:, c, :], banks[b][:, 0:256], ACT.Copy, scale=1.0 / 64, w=[t1, t])
                t3 = A.do(act, m2[:, c, :], banks[b][:, 0:256], ACT.Square, scale=1.0 / 64, w=[t1])
                t4 = V.do(stt, m2[:, c, :], banks[b][:, 256:512], 1.0 / 64, m2[:, c, :], ALU.mult,
                          ALU.subtract, w=[t3])
                give(b, [t4])
                if c % 2:
                    yield
            hv = (slice(0, 2), slice(2, 4))
            tm_ = [V.do(ts, m2[:, x, :], m2[:, x, :], 0.0, None, ALU.max, w=[t4]) for x in hv]
            t5 = [V.do(tt, m1[:, x, :], YT[:, x, :], m1[:, x, :], ALU.subtract, w=[t3]) for x in hv]
            t6 = []
            for i, x in enumerate(hv):
                k = A.do(act, m2[:, x, :], m2[:, x, :], ACT.Ln, bias=epsgn, w=[tm_[i]])
                t6.append(A.do(act, m2[:, x, :], m2[:, x, :], ACT.Exp, scale=-0.5, w=[k]))
            yield
            t7 = [V.do(tt, m1[:, x, :], m1[:, x, :], m2[:, x, :], ALU.mult, w=[t5[i], t6[i]])
                  for i, x in enumerate(hv)]
            t8 = [A.do(act, m1[:, c, :], m1[:, c, :], ACT.Identity, scale=col("rwkv_lnx_w", c),
                       bias=col("rwkv_lnx_b", c), w=[t7[c // 2]]) for c in range(4)]
            yield
            t9 = [V.do(tt, m1[:, x, :], m1[:, x, :], BON[:, x, :], ALU.add, w=[t8[1 + 2 * i], tbon])
                  for i, x in enumerate(hv)]
            t10 = []
            for u in range(2):
                yield from room(2)
                b, fr = take()
                P.wait(fr, tsg)
                for v in range(2):
                    c = 2 * u + v
                    t1 = P.do(mm, banks[b][:, 256 * v:256 * v + 256], SM("g2")[:, 128 * c:128 * c + 128], sg,
                              True, True)
                t10.append(V.do(tt, m1[:, hv[u], :], m1[:, hv[u], :],
                                banks[b][:, :].rearrange("p (v n) -> p v n", v=2), ALU.mult, w=[t9[u], t1]))
                give(b, [t10[u]])
            yield
            for u in range(2):
                k = halve(oaH[:, hv[u], :], oaL[:, hv[u], :], m1[:, hv[u], :], [t10[u], t])
                oa_tok += [k, k]
            R_["oa"] = oa_tok

        def soft1(qa, ka, bias, E, sc, deps, e_free, extra=None):
            b, fr = take()
            P.wait(fr, *deps)
            if extra is None:
                P.do(mm, banks[b][:, 0:128], qa[:, 0:128], ka[:, 0:128], True, True, inc=False)
                t = P.do(mm, banks[b][:, 128:384], qa[:, 128:256], ka[:, 0:256], True, True)
            else:
                t = extra(banks[b])
            r0 = V.do(ttr, E[:, 0:128], banks[b][:, 0:128], bias[:, 0:128], ALU.add, ALU.max, -3.0e38,
                      sc[:, 0:1], w=[t, e_free])
            r1 = V.do(ttr, E[:, 128:384], banks[b][:, 128:384], bias[:, 128:384], ALU.add, ALU.max, -3.0e38,
                      sc[:, 1:2], w=[t, e_free])
            give(b, [r0, r1])
            nm = V.do(ts, sc[:, 2:4], sc[:, 0:2], -1.0, None, ALU.mult, w=[r0, r1])
            e0 = A.do(act, E[:, 0:128], E[:, 0:128], ACT.Exp, bias=sc[:, 2:3], accum_out=sc[:, 4:5], w=[nm])
            e1 = A.do(act, E[:, 128:384], E[:, 128:384], ACT.Exp, bias=sc[:, 3:4], accum_out=sc[:, 5:6], w=[nm])
            return [e0, e1]

        def turn(E, ET, deps, et_free):
            b, fr = take()
            P.wait(fr, *deps)
            for i in range(3):
                t = P.do(tr, banks[b][:, 128 * i:128 * i + 128], E[:, 128 * i:128 * i + 128], ident, inc=(i == 2))
            k = A.do(acopy, ET[:, :], banks[b][:, 0:384], w=[t, et_free])
            give(b, [k])
            return t, k

        def pv(o, v0, v1, ET):
            P.do(mm, o, v0, ET[:, 0:256], True, False, inc=False)
            return P.do(mm, o[:, 128:256], v1, ET[:, 256:384], False, True)

        def projections_of_w_in():
            for c in RWKV_ORDER:
                yield from proj_t("w_in", 0, c, HH, HL, 256, 8, hdep, shift_evac)
            q_tok, k_tok, v_tok = [], [], []

            def diff_evac(o, c, t):
                n = (c - 1792) // 128
                if n < 4:
                    k = V.do(stt, qT[:, n:n + 2, :], o, 0.125, RB2, ALU.mult, ALU.mult, w=[t])
                    q_tok.append(k)
                else:
                    k = V.do(tt, kTt[:, n - 4:n - 2, :], o, RB2, ALU.mult, w=[t])
                    k_tok.append(k)
                return [k]

            for c in range(1792, 2816, 256):
                yield from proj_t("w_in", 0, c, HH, HL, 256, 8, hdep, diff_evac)

            def v_evac(o, b, h, t):
                k = A.do(act, vN[:, b, :], o, ACT.Copy, scale=rstd[b], w=[t, rdep])
                v_tok.append(k)
                return [k]

            yield from proj_n("w_in", 0, 8, 2816, 512, HH, HL, hdep, v_evac)
            R_["vd"] = q_tok, k_tok, v_tok
            ga_tok, gb_tok = [], []

            def ga_evac(o, c, t):
                n = (c - 3328) // 128
                ga_tok.append(V.do(tt, gA[:, n:n + 2, :], o, RB2, ALU.mult, w=[t, rdep]))
                return ga_tok[-1:]

            for c in range(3328, 4352, 256):
                yield from proj_t("w_in", 0, c, HH, HL, 256, 8, hdep, ga_evac)
            R_["sa"] = [A.do(act, gA[:, 4 * n:4 * n + 4, :], gA[:, 4 * n:4 * n + 4, :], ACT.Sigmoid, w=[ga_tok])
                        for n in range(2)]
            A.do(table, "natural_log_exp_and_others", inc=False)
            yield
            while "ob" not in R_:
                yield
            ob_tok, etf = R_["ob"], R_["etf"]

            def gb_evac(o, c, t):
                n = (c - 4352) // 128
                gb_tok.append(V.do(tt, gB[:, n:n + 2, :], o, RB2, ALU.mult, w=[t, ob_tok, etf]))
                return gb_tok[-1:]

            for c in range(4352, 5376, 256):
                yield from proj_t("w_in", 0, c, HH, HL, 256, 8, hdep, gb_evac)
            h_free[0] = last_pe()
            rb_free[0] = [ga_tok, gb_tok]
            sb_ = [A.do(act, gB[:, 4 * n:4 * n + 4, :], gB[:, 4 * n:4 * n + 4, :], ACT.Sigmoid, w=[gb_tok])
                   for n in range(2)]
            A.do(table, "natural_log_exp_and_others", inc=False)
            mb = R_["mb"] = {}

            def pb_evac(o, c, t):
                n = c // 128
                g = gB[:, n:n + 2, :]
                mb[n] = V.do(tt, g, o, g, ALU.mult, w=[t, sb_])
                return [mb[n]]

            for c in range(0, 1024, 512):
                yield from proj_t("w_proj_b", 0, c, obH, obL, 512, 4, ob_tok, pb_evac)

        def diff():
            while "vd" not in R_:
                yield
            q_tok, k_tok, v_tok = R_["vd"]
            while "u_start" not in R_:
                yield
            us = R_["u_start"]
            tl1 = V.do(ttr, oT[:, 0:64], SM("lam")[:, 0:64], SM("lam")[:, 64:128], ALU.mult, ALU.add, 0.0,
                       st[:, 40:41], w=[t_const, us])
            tl2 = V.do(ttr, oT[:, 0:64], SM("lam")[:, 128:192], SM("lam")[:, 192:256], ALU.mult, ALU.add, 0.0,
                       st[:, 41:42], w=[tl1])
            tl3 = A.do(act, st[:, 42:44], st[:, 40:42], ACT.Exp, w=[tl1, tl2])
            yield
            tl4 = V.do(tt, st[:, 44:45], st[:, 42:43], st[:, 43:44], ALU.subtract, w=[tl3])
            t_nlam = V.do(ts, st[:, 45:46], st[:, 44:45], 0.2, -1.0, ALU.add, ALU.mult, w=[tl4])
            ef, etf = us, us
            ob_tok = []
            tb = None
            scs = [st[:, 48 + 8 * c:56 + 8 * c] for c in range(2)]
            for h in range(4):
                ta_ = V.do(stt, AB[:, :], K("ndist"), 2.0 ** (-2.0 * (h + 1)), K("caus"), ALU.mult, ALU.add,
                           w=[t_const, us, tb])
                ee = []
                for c in range(2):
                    ee.append(soft1(qT[64 * c:64 * c + 64, h, :], kTt[64 * c:64 * c + 64, h, :], AB[:, :], Es[c],
                                    scs[c], [q_tok, k_tok], [ef, ta_]))
                    tb = V.n and (V.sem, V.n)
                    yield
                for c in range(2):
                    tn = V.do(rcp, scs[c][:, 6:8], scs[c][:, 4:6], w=[ee[c]])
                tn = V.do(ts, scs[1][:, 6:8], scs[1][:, 6:8], st[:, 45:46], None, ALU.mult, w=[tn, t_nlam])
                w_ = []
                for m, (a, z) in enumerate(((0, 128), (128, 384))):
                    t1 = V.do(ts, Es[1][:, a:z], Es[1][:, a:z], scs[1][:, 6 + m:7 + m], None, ALU.mult, w=[tn])
                    w_.append(V.do(stt, Es[0][:, a:z], Es[0][:, a:z], scs[0][:, 6 + m:7 + m], Es[1][:, a:z],
                                   ALU.mult, ALU.add, w=[t1]))
                yield
                tE, tET = turn(Es[0], ETs, [w_], [etf])
                ef = [tE]
                yield
                b, fr = take()
                P.wait(fr, tET, v_tok)
                t = pv(banks[b][:, 0:256], vN[:, 0, 128 * h:128 * h + 128], vN[:, 1, 128 * h:128 * h + 128], ETs)
                etf = [t]
                t1 = V.do(cp, oT[:, :], banks[b][:, 0:256], w=[t])
                t2 = A.do(act, sqd[:, :], banks[b][:, 0:256], ACT.Square, w=[t1])
                give(b, [t1, t2])
                yield
                b, fr = take()
                t3 = P.do(mm, banks[b][:, 0:256], K("ones128"), sqd[:, :], True, True, w=[fr, t2])
                t4 = A.do(act, sqd[:, :], banks[b][:, 0:256], ACT.Ln, scale=1.0 / 128, bias=epssub, w=[t3])
                give(b, [t4])
                t5 = A.do(act, sqd[:, :], sqd[:, :], ACT.Exp, scale=-0.5, w=[t4])
                yield
                t6 = V.do(tt, oT[:, :], oT[:, :], sqd[:, :], ALU.mult, w=[t1, t5])
                t7 = V.do(ts, oT[:, :], oT[:, :], col("diff_subln_g"), 0.8, ALU.mult, ALU.mult, w=[t6])
                ob_tok.append(halve(obH[:, h, :], obL[:, h, :], oT[:, :], [t7]))
                yield
            R_["etf"] = etf
            R_["ob"] = ob_tok

        R_["free"] = [rdep]
        run(rwkv(), diff(), fill=[projections_of_w_in()], lead=LEADS[0])

        oa_tok = R_["oa"]
        gar = Arena(16 * 1024)
        mH = gar([128, 8, S], R)
        mL = gar([128, 8, S], R)
        assert gar.here() <= keep
        m_tok = {}

        def pa_evac(o, c, t):
            n = c // 128
            g = gA[:, n:n + 2, :]
            t1 = V.do(tt, g, o, g, ALU.mult, w=[t, R_["sa"], oa_tok])
            t2 = V.do(tt, g, g, gB[:, n:n + 2, :], ALU.add, w=[t1, R_["mb"][n]])
            m_tok[n] = m_tok[n + 1] = halve(mH[:, n:n + 2, :], mL[:, n:n + 2, :], g, [t2])
            return [t1]

        for c in range(0, 1024, 512):
            run(fill=[proj_t("w_proj_a", 0, c, oaH, oaL, 512, 4, oa_tok, pa_evac)])
        for b in range(2):
            SP.dma(X[:, b, :], xin[:, b, :], s_x[b], w=[list(m_tok.values())])
            for h in range(2):
                xt[b, h] = [(s_x[b], 32)]
        nm = Norm("norm_mlp_g")
        run(proj_n("w_out", 0, 8, 0, 1024, mH, mL, m_tok, x_add(), 2, nm))


        def ff_bufs(n):
            a = Arena(0)
            return a([128, n, S], R), a([128, n, S], R), a

        sH, sL, fa = ff_bufs(32)
        rl = [fa([128, 2, S]) for _ in range(2)]
        hdep, rdep = nm.h, nm.r
        f_tok = {}
        rf = [None, None]

        def relu_evac(o, c, t):
            n = c // 128
            j = (n // 2) % 2
            t1 = V.do(stt, rl[j][:, :, :], o, 0.0, RB2, ALU.max, ALU.mult, w=[t, rf[j], rdep])
            t2 = A.do(act, sH[:, n:n + 2, :], rl[j][:, :, :], ACT.Square, w=[t1])
            t3 = V.do(tt, rl[j][:, :, :], rl[j][:, :, :], rl[j][:, :, :], ALU.mult, w=[t2])
            t4 = V.do(tt, sL[:, n:n + 2, :], rl[j][:, :, :], sH[:, n:n + 2, :].bitcast(F), ALU.subtract, w=[t3])
            rf[j] = t4
            f_tok[n] = f_tok[n + 1] = [t2, t4]
            rb_free[0] = [t1]
            return [t1]

        pr = fa([128, 2, S])
        pH = fa([128, 2, S], R)
        pL = fa([128, 2, S], R)
        plo = fa([128, 2, D])
        frow = fa([128, D])
        s_p = sem("s_p")
        SP.dma(pr[:, :, :], pin, s_p, w=[xt[0, 0]])
        SP.dma(frow[:, :], rowin, s_row, w=[xt[0, 0]])
        for c in range(0, 4096, 256):
            run(proj_t("w_ff1", 0, c, HH, HL, 256, 8, hdep, relu_evac))
        h_free[0] = last_pe()
        ptok = halve(pH[:, :, :], pL[:, :, :], pr[:, :, :], [(s_p, 16)])
        plotok = {}

        def ple_evac(o, b, h, t):
            k = A.do(acopy, plo[:, b, 512 * h:512 * h + 512], o, w=[t])
            plotok[b, h] = k
            return [k]

        nm = Norm("norm_ple_g")
        run(proj_n("w_ff2", 0, 32, 0, 1024, sH, sL, f_tok, x_add(), 1, nm,
                   proj_n("w_ple", 0, 2, 0, 1024, pH, pL, [ptok, ptok], ple_evac)))

        sgt = Arena(0)([128, 2, D])
        hdep, rdep = nm.h, nm.r

        def sg_evac(o, b, h, t):
            g = sgt[:, b, 512 * h:512 * h + 512]
            xb = X[:, b, 512 * h:512 * h + 512]
            k = A.do(act, g, o, ACT.Sigmoid, scale=rstd[b], w=[t, rdep])
            rb_free[0] = [k]
            t1 = V.do(tt, g, plo[:, b, 512 * h:512 * h + 512], g, ALU.mult, w=[k, plotok[b, h]])
            xt[b, h] = [V.do(tt, xb, xb, g, ALU.add, w=[t1, xt[b, h]])]
            return [k]

        nm = FinalNorm("norm_ffn1_2", frow, (s_row, 16))
        h_free[0] = None
        run(proj_n("w_ple_gate", 0, 8, 0, 1024, HH, HL, hdep, sg_evac, 2, nm))

        def swiglu(n, layer, nm, nxt):
            aH, aL, fa_ = ff_bufs(22)
            sgm = [fa_([128, 2, S]) for _ in range(2)]
            sgs = [fa_([128, 2, S]) for _ in range(2)]
            hdep, rdep = nm.h, nm.r
            gfr = [None, None]
            toks = {}
            held = {}

            def g_evac(o, c, t):
                j = (c // 256) % 2
                t1 = V.do(tt, sgm[j][:, :, :], o, RB2, ALU.mult, w=[t, gfr[j], rdep])
                t2 = A.do(act, sgs[j][:, :, :], sgm[j][:, :, :], ACT.Sigmoid, w=[t1, gfr[j]])
                held[c] = t2
                return [t1]

            def u_evac(o, c, t):
                j = (c // 256) % 2
                m = c // 128
                t0 = V.do(tt, sgm[j][:, :, :], sgm[j][:, :, :], sgs[j][:, :, :], ALU.mult, w=[held[c]])
                t1 = V.do(tt, sgs[j][:, :, :], o, RB2, ALU.mult, w=[t, t0])
                t1b = V.do(tt, sgm[j][:, :, :], sgm[j][:, :, :], sgs[j][:, :, :], ALU.mult, w=[t1])
                k = halve(aH[:, m:m + 2, :], aL[:, m:m + 2, :], sgm[j][:, :, :], [t1b])
                gfr[j] = k
                toks[m] = toks[m + 1] = k
                rb_free[0] = [t1]
                return [t1]

            for c in range(0, 2816, 256):
                run(proj_t(f"ffn{n}_w_gate_2", layer, c, HH, HL, 256, 8, hdep, g_evac))
                run(proj_t(f"ffn{n}_w_up_2", layer, c, HH, HL, 256, 8, hdep, u_evac))
            h_free[0] = last_pe()
            run(proj_n(f"ffn{n}_w_down_2", layer, 22, 0, 1024, aH, aL, toks, x_add(0.5), 2, nxt))

        def attention(layer, nm, nxt):
            a_ = Arena(0)
            mH_ = a_([128, 8, S], R)
            mL_ = a_([128, 8, S], R)
            Q = a_([128, 8, S])
            KK = a_([128, 8, S])
            VV = a_([128, 2, D])
            w8s = [[a_([128, 2, 512]) for _ in range(3)] for _ in range(2)]
            hdep, rdep = nm.h, nm.r
            qtok, ktok, vtok = {0: [], 4: []}, {0: [], 4: []}, []
            wf = [None, None]

            def rope_tabs(gname, gsname):
                g = a_([128, 2, 64])
                gs = a_([128, 2, 64])
                c_ = K("cos").rearrange("p (b d) -> p b d", b=2)
                s_ = K("sin").rearrange("p (b d) -> p b d", b=2)
                for b in range(2):
                    V.do(tt, g[:, b, :], c_[:, b, :], SM(gname), ALU.mult)
                    t = V.do(tt, gs[:, b, :], s_[:, b, :], SM(gsname), ALU.mult)
                return g, gs, t

            todo = []

            def qk_norm(j, held, g, gs, dst, tk, scale):
                sqb, qn, q2 = w8s[j]
                q4, z4, s3 = (x[:, :, :].rearrange("p b (h d) -> p b h d", h=8) for x in (qn, q2, sqb))
                s0 = 224 + 64 * j
                ss, sy, sz, sr = (st[:, i:i + 16] for i in range(s0, s0 + 64, 16))
                ta = [A.do(act, sqb[:, b, :], banks[i][:, :], ACT.Square, scale=rstd[b], w=[t, rdep])
                      for b, (i, t) in enumerate(held)]
                split_lo()
                t2 = [V.do(red, ss[:, 8 * b:8 * b + 8], s3[:, b, :, :], ALU.add, w=[ta[b]]) for b in range(2)]
                yield
                t2 = V.do(ts, ss, ss, 1.0 / 64, EPS, ALU.mult, ALU.add, w=t2)
                t3 = A.do(act, sy, ss, ACT.Ln, w=[t2])
                t3 = A.do(act, sy, sy, ACT.Exp, scale=-0.5, w=[t3])
                yield
                t3 = newton(sy, ss, sz, sr, [t3])
                t4 = []
                for b, (i, t) in enumerate(held):
                    t4.append(V.do(stt, q4[:, b, :, :], banks[i][:, :].rearrange("p (h d) -> p h d", h=8), rstd[b],
                                   bc(sr[:, 8 * b:8 * b + 8].rearrange("p (h o) -> p h o", o=1), 2, 64), ALU.mult,
                                   ALU.mult, w=[t3, wf[j]]))
                    give(i, [ta[b], t4[b]])
                yield

                def tab(x):
                    return bc(x.rearrange("p b (o d) -> p b o d", o=1), 2, 8)
                if gs is None:
                    g_ = bc(bc(g.rearrange("p (b o d) -> p b o d", b=1, o=1), 1, 2), 2, 8)
                    t5 = V.do(tt, q4, q4, g_, ALU.mult, w=[t4])
                else:
                    t6 = V.do(tt, z4[:, :, :, 0:32], q4[:, :, :, 32:64], tab(gs[:, :, 0:32]), ALU.mult, w=[t4])
                    t7 = V.do(tt, z4[:, :, :, 32:64], q4[:, :, :, 0:32], tab(gs[:, :, 32:64]), ALU.mult, w=[t4])
                    yield
                    t8 = V.do(tt, q4, q4, tab(g[:, :, :]), ALU.mult, w=[t6, t7])
                    t5 = V.do(tt, q4, q4, z4, ALU.add, w=[t8])

                def finish():
                    for b in range(2):
                        bb, fr = take()
                        P.wait(fr, t5)
                        for c in range(4):
                            tp = P.do(tr, banks[bb][:, 128 * c:128 * c + 128], qn[:, b, 128 * c:128 * c + 128],
                                      ident, inc=(c == 3))
                        k = A.do(act, dst[:, :, 128 * b:128 * b + 128], b4(bb), ACT.Copy, scale=scale, w=[tp])
                        give(bb, [k])
                        tk.append(k)
                        wf[j] = tp
                yield
                yield from room(1)
                finish()

            def vv_evac(o, b, h, t):
                k = A.do(act, VV[:, b, 512 * h:512 * h + 512], o, ACT.Copy, scale=rstd[b], w=[t, rdep])
                vtok.append(k)
                return [k]

            if layer == 0:
                def a_evac(dst, tk, c0, scale):
                    def f(o, c, t):
                        n = (c - c0) // 128
                        k = V.do(stt, dst[:, n:n + 2, :], o, scale, RB2, ALU.mult, ALU.mult, w=[t, rdep])
                        tk[0].append(k)
                        return [k]
                    return f
                f1, f2 = a_evac(Q, qtok, 0, 0.125), a_evac(KK, ktok, 1024, 1.0)
                for c in range(0, 512, 256):
                    run(proj_t("w_in_ab_2", 0, c, HH, HL, 256, 8, hdep, f1))
                for c in range(1024, 1536, 256):
                    run(proj_t("w_in_ab_2", 0, c, HH, HL, 256, 8, hdep, f2))
                wn = "w_in_ab_2"
                gq, gqs, tg = rope_tabs("gq", "gqs")
                gk, gks, tg2 = rope_tabs("gk", "gks")
                jobs = [(512, Q, qtok, gq, gqs, 0.125, 4), (1536, KK, ktok, gk, gks, 1.0, 4)]
                early = []
            else:
                wn = "w_in_cd_2"
                gq, gqs, tg = rope_tabs("gqd", "gqds")
                gk, gks, tg2 = rope_tabs("gkd", "gkds")
                early = [(0, Q, qtok, None, None, 0.125, 0), (1024, KK, ktok, None, None, 1.0, 0)]
                jobs = [(512, Q, qtok, gq, gqs, 0.125, 4), (1536, KK, ktok, gk, gks, 1.0, 4)]

            def qk(jobs_):
                for c, dst, tk, g, gs, scale, n0 in jobs_:
                    held = []

                    def q_evac(o, b, h, t):
                        held.append((cur_bank[0], t))
                        if b == 1:
                            ga = SM("gqc") if g is None and dst is Q else SM("gkc") if g is None else g
                            todo.append((held, ga, gs, dst[:, n0:n0 + 4, :], tk[n0], scale))
                        return None
                    yield from room(3)
                    yield from proj_n(wn, 0, 8, c, 512, HH, HL, hdep, q_evac)

            def norms(j):
                for n in range(j, len(early + jobs), 2):
                    while len(todo) <= n:
                        yield
                    yield from qk_norm(j, *todo[n])
                    yield

            def projections():
                yield from qk(early)
                if layer == 1:
                    yield from forget()
                yield from qk(jobs)
                while len(free) < 5:
                    yield
                yield from proj_n(wn, 0, 8, 2048, 1024, HH, HL, hdep, vv_evac)
                h_free[0] = last_pe()
                rb_free[0] = [last_va()]
                yield from room(5)
                yield from proj_n("w_out_2", layer, 8, 0, 1024, mH_, mL_, mtok, x_add(), 1, nxt)

            def last_va():
                return [(V.sem, V.n), (A.sem, A.n)]

            ctok = []
            if layer == 1:
                cf = a_([8, 2, S])
                wfh = a_([128, 64], R)
                wfl = a_([128, 64], R)

            def forget():
                f1 = halve(wfh[:, :], wfl[:, :], SM("wf"), [])
                b, fr = take()
                P.wait(fr, f1, [need(d) for d in hdep.values()])
                o = banks[b][0:8, 0:256]
                for k in range(8):
                    t = mm3(o, wfh[:, 8 * k:8 * k + 8], wfl[:, 8 * k:8 * k + 8], HH[:, k, :], HL[:, k, :],
                            k == 0, k == 7)
                z, e = cf[:, 0, :], cf[:, 1, :]
                t1 = V.do(tt, z, o, RB[0:8, :], ALU.mult, w=[t, rdep])
                give(b, [t1])
                yield
                t1 = V.do(ts, z, z, SM("bf", 0, 8), None, ALU.add, w=[t1])
                t2 = A.do(act, e, z, ACT.Abs, w=[t1])
                t3 = A.do(act, e, e, ACT.Exp, scale=-1.0, w=[t2])
                t3 = A.do(act, e, e, ACT.Ln, bias=one1[0:8, :], w=[t3])
                t4 = V.do(stt, z, z, 0.0, e, ALU.min, ALU.subtract, w=[t3])
                t5 = V.do(scan, e, bc(K("ones128", 8)[:, 0:1], 1, 256), z, 0.0, ALU.mult, ALU.add, w=[t4])
                t6 = V.do(ts, z, e, -1.0, None, ALU.mult, w=[t5])
                ctok.extend([t5, t6])
                yield
            NE = DEPTH
            Eb = [a_([128, 384]) for _ in range(NE)]
            ETb = [a_([128, 384]) for _ in range(NE)]
            ef_, etf_ = [None] * NE, [None] * NE
            mtok = {}
            obank = {}
            over = set()

            def head(h, n0):
                m, p0 = h // 2, 64 * (h % 2)
                qa, ka = Q[p0:p0 + 64, m, :], KK[p0:p0 + 64, m, :]
                i = h % NE
                E, ET = Eb[i], ETb[i]
                sc = st[:, 176 + 8 * i:184 + 8 * i]
                while h >= NE and h - NE not in over:
                    yield
                while not (len(qtok[n0]) >= 2 and len(ktok[n0]) >= 2 and (ctok or layer == 0)):
                    yield
                qd = [qtok[n0], ktok[n0]]
                if layer == 0 and h < 8:
                    yield from room(2)
                    b, fr = take()
                    P.wait(fr, qd)
                    P.do(mm, banks[b][:, 0:256], ka[:, 0:128], qa[:, 0:256], True, True, inc=False)
                    t = P.do(mm, banks[b][:, 256:384], ka[:, 128:256], qa[:, 128:256], True, True)
                    z = banks[b][:, 0:384]
                    t0 = A.do(acopy, ET[:, :], z, w=[t, etf_[i]])
                    give(b, [t0])
                    t1 = A.do(act, E[:, :], ET[:, :], ACT.Abs, w=[t0, ef_[i]])
                    t2 = A.do(act, E[:, :], E[:, :], ACT.Exp, scale=-1.0, w=[t1])
                    t2 = A.do(act, E[:, :], E[:, :], ACT.Ln, bias=one1, w=[t2])
                    yield
                    t3 = V.do(stt, E[:, :], ET[:, :], 0.0, E[:, :], ALU.max, ALU.add, w=[t2])
                    t4 = V.do(tt, E[:, 0:128], E[:, 0:128], K("strict"), ALU.mult, w=[t3])
                    t5 = V.do(tt, E[:, 256:384], E[:, 256:384], K("strict"), ALU.mult, w=[t3])
                    yield
                    yield from room(2)
                    b2, fr2 = take()
                    P.wait(fr2)
                    o = banks[b2]
                    P.do(mm, o[:, 0:256], K("ntri"), E[:, 0:256], True, False, w=[t4, t5], inc=False)
                    P.do(mm, o[:, 128:256], K("nones"), E[:, 256:384], False, True, inc=False)
                    t6 = P.do(mm, o[:, 256:384], K("ntri"), E[:, 256:384], True, True)
                    ef_[i] = t6
                    t6b = V.do(tt, ET[:, :], ET[:, :], o[:, 0:384], ALU.add, w=[t6])
                    give(b2, [t6b])
                    t7 = A.do(act, ET[:, :], ET[:, :], ACT.Exp, w=[t6b])
                    yield
                    t8 = V.do(tt, ET[:, 0:128], ET[:, 0:128], K("strict"), ALU.mult, w=[t7])
                    t9 = V.do(tt, ET[:, 256:384], ET[:, 256:384], K("strict"), ALU.mult, w=[t7])
                    et = [t7, t8, t9]
                else:
                    bias = K("dil") if (layer == 1 and h >= 8) else K("caus")
                    extra = None
                    if layer == 1 and h < 8:
                        selh = bc(K("ident", 8)[:, h:h + 1], 1, 128)
                        c_, nc_ = cf[:, 1, :], cf[:, 0, :]

                        def extra(bank):
                            for q, (a0, a1) in enumerate(((0, 128), (128, 384))):
                                w_ = a1 - a0
                                o = bank[:, a0:a1]
                                P.do(mm, o, qa[:, 128 * q:128 * q + 128], ka[:, 0:w_], True, False, inc=False)
                                P.do(mm, o, selh, nc_[:, 0:w_], False, False, inc=False)
                                for u in range(w_ // 128):
                                    t = P.do(mm, o[:, 128 * u:128 * u + 128], c_[:, 128 * q:128 * q + 128], selh,
                                             False, u == w_ // 128 - 1)
                            return t
                    yield from room(2)
                    e_ = soft1(qa, ka, bias, E, sc, [qd, ctok], [ef_[i]], extra)
                    yield
                    r_ = V.do(rcp, sc[:, 6:8], sc[:, 4:6], w=[e_])
                    n0_ = V.do(ts, E[:, 0:128], E[:, 0:128], sc[:, 6:7], None, ALU.mult, w=[r_])
                    n1_ = V.do(ts, E[:, 128:384], E[:, 128:384], sc[:, 7:8], None, ALU.mult, w=[r_])
                    yield
                    yield from room(2)
                    tE, tET = turn(E, ET, [n0_, n1_], [etf_[i]])
                    ef_[i] = tE
                    et = [tET]
                yield
                while len(vtok) < 4:
                    yield
                if m not in obank:
                    yield from room(2)
                if m not in obank:
                    obank[m] = take()
                ob = obank[m]
                P.wait(et, vtok, ob[1])
                o = banks[ob[0]][p0:p0 + 64, 0:256]
                t = pv(o, VV[:, 0, 64 * h:64 * h + 64], VV[:, 1, 64 * h:64 * h + 64], ET)
                etf_[i] = t
                obank.setdefault(("done", m), []).append(t)
                if len(obank[("done", m)]) == 2:
                    b = ob[0]
                    k1 = A.do(acopy, mH_[:, m, :], banks[b][:, 0:256], w=[obank[("done", m)]])
                    k2 = V.do(tt, mL_[:, m, :], banks[b][:, 0:256], mH_[:, m, :].bitcast(F), ALU.subtract, w=[k1])
                    give(b, [k1, k2])
                    mtok[m] = [k1, k2]
                over.add(h)
                yield

            run(norms(0), norms(1), fill=[projections()], pool=[head(h, 0 if h < 8 else 4) for h in range(16)], depth=DEPTH, lead=LEADS[1 + layer])

        for layer in range(2):
            n1, n2 = Norm("norm_mix_2", 8 * layer), Norm("norm_ffn2_2", 8 * layer)
            swiglu(1, layer, nm, n1)
            attention(layer, n1, n2)
            nm = Norm("norm_ffn1_2", 8 * layer + 8) if layer == 0 else None
            swiglu(2, layer, n2, nm)

        for b in range(2):
            for h in range(2):
                o = slice(512 * h, 512 * h + 512)
                SP.dma(out[:, b, o], X[:, b, o], s_out, w=[xt[b, h]])
        SP.wait((s_out, 64))

        block = ctx.enter_context(nc.Block())

        @block.sync
        def _(e):
            SP.replay(e)

        @block.gpsimd
        def _(e):
            G.replay(e)

        @block.scalar
        def _(e):
            A.replay(e)

        @block.vector
        def _(e):
            V.replay(e)

        @block.tensor
        def _(e):
            P.replay(e)


def kernel(**inputs):
    import concourse.bacc as bacc
    from concourse.bass_utils import run_bass_kernel_spmd as run

    a = {k: np.asarray(v) for k, v in inputs.items()}
    plan = stream_plan()
    ws = np.empty((len(plan), 128, PIECE), np.float32)
    for i, (name, layer, k0, nk, c0, w) in enumerate(plan):
        m = a[name][layer][128 * k0:128 * (k0 + nk), c0:c0 + w]
        ws[i] = m.reshape(nk, 128, w).transpose(1, 0, 2).reshape(128, PIECE)
    CA, ncol = col_at()
    cols = np.concatenate([a[n].reshape(w, 128) for n, w in COLS], 0).T
    SA, ns = small_at()
    small = np.zeros((128, ns), np.float32)

    def put(name, v, r0=0):
        o, w = SA[name]
        v = v.reshape(-1, w)
        small[r0:r0 + (128 if v.shape[0] == 1 else v.shape[0]), o:o + w] = v

    put("lam", np.concatenate([a["lam_q1"][0], a["lam_k1"][0], a["lam_q2"][0], a["lam_k2"][0]]))
    for n, src in (("gq", "g_q_b_2"), ("gk", "g_k_b_2"), ("gqd", "g_q_d_2"), ("gkd", "g_k_d_2")):
        g = a[src][0]
        put(n, g)
        put(n + "s", np.concatenate([g[32:], g[:32]]))
    put("gqc", a["g_q_c_2"][0])
    put("gkc", a["g_k_c_2"][0])
    put("w2a2", np.concatenate([a["rwkv_w2"][0], a["rwkv_a2"][0]], 0))
    put("g2", a["rwkv_g2"][0])
    put("wf", a["w_in_cd_2"][0][:, 3072:3080].reshape(8, 128, 8).transpose(1, 0, 2).reshape(128, 64))
    put("bf", a["b_f_2"][0].reshape(8, 1))
    arrays = {
        "ws": ws,
        "xin": np.ascontiguousarray(a["x"][0].reshape(2, 128, D).transpose(1, 0, 2)),
        "pin": np.ascontiguousarray(a["p"][0, 0].T.reshape(2, 128, S).transpose(1, 0, 2)),
        "cols": np.ascontiguousarray(cols),
        "const": constants(),
        "small": small,
        "row": np.ascontiguousarray(np.broadcast_to(a["final_norm_g"], (128, D))),
    }
    nc = bacc.Bacc("TRN2", target_bir_lowering=False, num_devices=1)
    aps = [nc.dram_tensor(n, v.shape, mybir.dt.from_np(v.dtype), kind="ExternalInput").ap()
           for n, v in arrays.items()]
    out = nc.dram_tensor("out", (128, 2, D), F, kind="ExternalOutput").ap()
    program(nc, *aps, out)
    r = run(nc, [arrays], core_ids=[0])
    o = r.results[0]["out"]
    return o.transpose(1, 0, 2).reshape(1, S, D)
```
